# Optimizing a Trainium2 kernel written in Bass

```python
import math
import jax, jax.numpy as jnp
from jax import lax
import numpy as np

D_MODEL = 1024
BATCH = 1
SEQ = 1024
DEPTH = 2

D_MIX = 2 * D_MODEL
N_GROUPS = 4
GROUP_W = D_MIX // N_GROUPS
HEAD_DIM = 64
N_HEADS = GROUP_W // HEAD_DIM
EPS = 1e-6

GLA_DK = HEAD_DIM // 2
GLA_DV = HEAD_DIM
GLA_RANK = 16
GLA_NORMALIZER = 16.0
GLA_CHUNK = 64

Q_BLOCK = 128

MLA_Q_RANK = D_MODEL // 4
MLA_KV_RANK = D_MODEL // 8
MLA_NOPE = HEAD_DIM
MLA_ROPE = HEAD_DIM // 2
MLA_V = HEAD_DIM
ROPE_THETA = 10000.0

LRU_BLOCKS = N_HEADS
LRU_BW = GROUP_W // LRU_BLOCKS
CONV_W = 4
LRU_C = 8.0

IN_SIZES = (
    D_MIX,
    N_HEADS * GLA_DK, N_HEADS * GLA_DK,
    N_HEADS * GLA_DV, GLA_RANK,
    GROUP_W, GROUP_W, GROUP_W, N_HEADS,
    MLA_Q_RANK, MLA_KV_RANK, MLA_ROPE,
    GROUP_W,
)
D_IN = sum(IN_SIZES)

kernel_name = "hymba_style_gla_fox_mla_rglru"

def rms_norm(x, g):
    xf = x.astype(jnp.float32)
    y = xf * lax.rsqrt(jnp.mean(xf * xf, axis=-1, keepdims=True) + EPS)
    return (y * g.astype(jnp.float32)).astype(x.dtype)

def split_heads(z, d):
    return z.reshape(z.shape[0], z.shape[1], -1, d)

def gla_mixer(q, k, v, g_in, w_up, b_up, g_out):
    B_, T, _ = q.shape
    nc = T // GLA_CHUNK
    f32 = jnp.float32
    log_a = jax.nn.log_sigmoid((g_in.astype(f32) @ w_up.astype(f32)) + b_up.astype(f32)) / GLA_NORMALIZER

    def chunks(z, d):
        return z.astype(f32).reshape(B_, nc, GLA_CHUNK, N_HEADS, d).transpose(1, 0, 3, 2, 4)

    qc = chunks(q, GLA_DK) * (GLA_DK ** -0.5)
    kc, vc, gc = chunks(k, GLA_DK), chunks(v, GLA_DV), chunks(log_a, GLA_DK)
    causal = jnp.tril(jnp.ones((GLA_CHUNK, GLA_CHUNK), dtype=bool))[:, :, None]

    def step(S, inp):
        q_, k_, v_, g_ = inp
        G = jnp.cumsum(g_, axis=2)
        o_inter = jnp.einsum('bhtk,bhkv->bhtv', q_ * jnp.exp(G), S)
        diff = G[:, :, :, None, :] - G[:, :, None, :, :]
        decay = jnp.exp(jnp.where(causal, diff, -jnp.inf))
        A = jnp.sum(q_[:, :, :, None, :] * k_[:, :, None, :, :] * decay, axis=-1)
        o = o_inter + jnp.einsum('bhts,bhsv->bhtv', A, v_)
        G_last = G[:, :, -1:, :]
        S_new = jnp.exp(G_last[:, :, 0, :])[..., None] * S + jnp.einsum('bhsk,bhsv->bhkv', k_ * jnp.exp(G_last - G), v_)
        return S_new, o

    S0 = jnp.zeros((B_, N_HEADS, GLA_DK, GLA_DV), f32)
    _, o = lax.scan(step, S0, (qc, kc, vc, gc))
    o = o.transpose(1, 0, 3, 2, 4).reshape(B_, T, N_HEADS, GLA_DV)
    o = rms_norm(o, g_out)
    return o.reshape(B_, T, N_HEADS * GLA_DV).astype(q.dtype)

def causal_block_attention(q, k, v, log_decay_cum=None):
    T = q.shape[1]
    scale = q.shape[-1] ** -0.5
    if log_decay_cum is not None:
        cum = jnp.transpose(log_decay_cum, (0, 2, 1))
    outs = []
    for blk in range(T // Q_BLOCK):
        lo, hi = blk * Q_BLOCK, (blk + 1) * Q_BLOCK
        s = jnp.einsum('bqhd,bkhd->bhqk', q[:, lo:hi], k[:, :hi]) * scale
        if log_decay_cum is not None:
            s = s + (cum[:, :, lo:hi, None] - cum[:, :, None, :hi])
        mask = (lo + jnp.arange(Q_BLOCK))[:, None] >= jnp.arange(hi)[None, :]
        p = jax.nn.softmax(jnp.where(mask, s, -jnp.inf), axis=-1)
        outs.append(jnp.einsum('bhqk,bkhd->bqhd', p, v[:, :hi]))
    return jnp.concatenate(outs, axis=1)

def fox_mixer(q, k, v, f_logit, b_f, g_q, g_k):
    B_, T, _ = q.shape
    f32 = jnp.float32
    qh = rms_norm(split_heads(q, HEAD_DIM), g_q).astype(f32)
    kh = rms_norm(split_heads(k, HEAD_DIM), g_k).astype(f32)
    vh = split_heads(v, HEAD_DIM).astype(f32)
    log_f = jax.nn.log_sigmoid(f_logit.astype(f32) + b_f.astype(f32))
    cum = jnp.cumsum(log_f, axis=1)
    o = causal_block_attention(qh, kh, vh, cum)
    return o.reshape(B_, T, GROUP_W).astype(q.dtype)

def apply_rope(z, positions):
    half = MLA_ROPE // 2
    inv_freq = ROPE_THETA ** (-jnp.arange(half, dtype=jnp.float32) / half)
    ang = positions.astype(jnp.float32)[:, :, None, None] * inv_freq
    cos, sin = jnp.cos(ang), jnp.sin(ang)
    z1, z2 = z[..., :half], z[..., half:]
    return jnp.concatenate([z1 * cos - z2 * sin, z1 * sin + z2 * cos], axis=-1)

def mla_mixer(c_q, c_kv, k_rope, positions, g_cq, w_uq, g_ckv, w_ukv, g_q, g_k):
    B_, T, _ = c_q.shape
    f32 = jnp.float32
    q = split_heads(rms_norm(c_q, g_cq) @ w_uq, MLA_NOPE + MLA_ROPE)
    kv = split_heads(rms_norm(c_kv, g_ckv) @ w_ukv, MLA_NOPE + MLA_V)
    k_nope, v = kv[..., :MLA_NOPE], kv[..., MLA_NOPE:]
    k_r = jnp.broadcast_to(k_rope[:, :, None, :], (B_, T, N_HEADS, MLA_ROPE))
    k = jnp.concatenate([k_nope, k_r.astype(k_nope.dtype)], axis=-1)
    q = rms_norm(q, g_q).astype(f32)
    k = rms_norm(k, g_k).astype(f32)
    q = jnp.concatenate([q[..., :MLA_NOPE], apply_rope(q[..., MLA_NOPE:], positions)], axis=-1)
    k = jnp.concatenate([k[..., :MLA_NOPE], apply_rope(k[..., MLA_NOPE:], positions)], axis=-1)
    o = causal_block_attention(q, k, v.astype(f32))
    return o.reshape(B_, T, N_HEADS * MLA_V).astype(c_q.dtype)

def rglru_mixer(xb, conv_w, conv_b, w_r, b_r, w_i, b_i, lam):
    B_, T, C = xb.shape
    f32 = jnp.float32
    xc = lax.conv_general_dilated(
        xb.astype(f32), conv_w.astype(f32)[:, None, :], window_strides=(1,), padding=[(CONV_W - 1, 0)],
        dimension_numbers=('NWC', 'WIO', 'NWC'), feature_group_count=C) + conv_b.astype(f32)
    xg = xc.reshape(B_, T, LRU_BLOCKS, LRU_BW)
    r = jax.nn.sigmoid(jnp.einsum('btnc,ncd->btnd', xg, w_r.astype(f32)).reshape(B_, T, C) + b_r.astype(f32))
    i = jax.nn.sigmoid(jnp.einsum('btnc,ncd->btnd', xg, w_i.astype(f32)).reshape(B_, T, C) + b_i.astype(f32))
    log_a = -LRU_C * r * jax.nn.softplus(-lam.astype(f32))
    a = jnp.exp(log_a)
    bx = jnp.sqrt(-jnp.expm1(2.0 * log_a)) * (i * xc)

    def combine(e1, e2):
        a1, b1 = e1
        a2, b2 = e2
        return a1 * a2, a2 * b1 + b2

    _, h = lax.associative_scan(combine, (a, bx), axis=1)
    return h.astype(xb.dtype)

def hybrid_layer(x, positions, norm_g, w_in, w_out, gla_w_up, gla_b_up, gla_g_out, fox_b_f, fox_g_q, fox_g_k,
                 mla_g_cq, mla_w_uq, mla_g_ckv, mla_w_ukv, mla_g_q, mla_g_k,
                 lru_conv_w, lru_conv_b, lru_w_r, lru_b_r, lru_w_i, lru_b_i, lru_lam):
    h = rms_norm(x, norm_g)
    proj = h @ w_in
    points = np.cumsum(np.array(IN_SIZES))[:-1].tolist()
    (gate, a_q, a_k, a_v, a_g, b_q, b_k, b_v, b_f, c_q, c_kv, c_kr, d_x) = jnp.split(proj, points, axis=-1)
    ya = gla_mixer(a_q, a_k, a_v, a_g, gla_w_up, gla_b_up, gla_g_out)
    yb = fox_mixer(b_q, b_k, b_v, b_f, fox_b_f, fox_g_q, fox_g_k)
    yc = mla_mixer(c_q, c_kv, c_kr, positions, mla_g_cq, mla_w_uq, mla_g_ckv, mla_w_ukv, mla_g_q, mla_g_k)
    yd = rglru_mixer(d_x, lru_conv_w, lru_conv_b, lru_w_r, lru_b_r, lru_w_i, lru_b_i, lru_lam)
    y = jnp.concatenate([ya, yb, yc, yd], axis=-1).astype(proj.dtype) * jax.nn.silu(gate)
    return x + (y @ w_out).astype(x.dtype)

def setup_inputs(seed: int = 0) -> dict:
    key = jax.random.key(seed)
    ks = jax.random.split(key, 32)
    f32 = jnp.float32

    def nrm(k, shape, fan_in):
        return jax.random.normal(k, shape, f32) * fan_in ** -0.5

    def gain(k, shape):
        return 1.0 + 0.05 * jax.random.normal(k, shape, f32)

    def bias(k, shape):
        return 0.02 * jax.random.normal(k, shape, f32)

    L = DEPTH
    x = jax.random.normal(ks[0], (BATCH, SEQ, D_MODEL), f32)
    offset = jax.random.randint(ks[1], (BATCH, 1), 0, 1024, dtype=jnp.int32)
    positions = offset + jnp.arange(SEQ, dtype=jnp.int32)[None, :]
    u = jax.random.uniform(ks[23], (L, GROUP_W), f32, 0.9, 0.999)
    a0 = u ** (1.0 / LRU_C)
    lru_lam = jnp.log(a0) - jnp.log1p(-a0)
    return {
        "x": x,
        "positions": positions,
        "norm_g": gain(ks[2], (L, D_MODEL)),
        "w_in": nrm(ks[3], (L, D_MODEL, D_IN), D_MODEL),
        "w_out": nrm(ks[4], (L, D_MIX, D_MODEL), D_MIX),
        "gla_w_up": nrm(ks[5], (L, GLA_RANK, N_HEADS * GLA_DK), GLA_RANK),
        "gla_b_up": bias(ks[6], (L, N_HEADS * GLA_DK)),
        "gla_g_out": gain(ks[7], (L, GLA_DV)),
        "fox_b_f": jax.random.uniform(ks[8], (L, N_HEADS), f32, 1.0, 4.0),
        "fox_g_q": gain(ks[9], (L, HEAD_DIM)),
        "fox_g_k": gain(ks[10], (L, HEAD_DIM)),
        "mla_g_cq": gain(ks[11], (L, MLA_Q_RANK)),
        "mla_w_uq": nrm(ks[12], (L, MLA_Q_RANK, N_HEADS * (MLA_NOPE + MLA_ROPE)), MLA_Q_RANK),
        "mla_g_ckv": gain(ks[13], (L, MLA_KV_RANK)),
        "mla_w_ukv": nrm(ks[14], (L, MLA_KV_RANK, N_HEADS * (MLA_NOPE + MLA_V)), MLA_KV_RANK),
        "mla_g_q": gain(ks[15], (L, MLA_NOPE + MLA_ROPE)),
        "mla_g_k": gain(ks[16], (L, MLA_NOPE + MLA_ROPE)),
        "lru_conv_w": nrm(ks[17], (L, CONV_W, GROUP_W), CONV_W),
        "lru_conv_b": bias(ks[18], (L, GROUP_W)),
        "lru_w_r": nrm(ks[19], (L, LRU_BLOCKS, LRU_BW, LRU_BW), LRU_BW),
        "lru_b_r": bias(ks[20], (L, GROUP_W)),
        "lru_w_i": nrm(ks[21], (L, LRU_BLOCKS, LRU_BW, LRU_BW), LRU_BW),
        "lru_b_i": bias(ks[22], (L, GROUP_W)),
        "lru_lam": lru_lam,
    }

def reference(x, positions, norm_g, w_in, w_out, gla_w_up, gla_b_up, gla_g_out, fox_b_f, fox_g_q, fox_g_k,
              mla_g_cq, mla_w_uq, mla_g_ckv, mla_w_ukv, mla_g_q, mla_g_k,
              lru_conv_w, lru_conv_b, lru_w_r, lru_b_r, lru_w_i, lru_b_i, lru_lam):
    for l in range(DEPTH):
        x = hybrid_layer(x, positions, norm_g[l], w_in[l], w_out[l], gla_w_up[l], gla_b_up[l], gla_g_out[l],
                         fox_b_f[l], fox_g_q[l], fox_g_k[l], mla_g_cq[l], mla_w_uq[l], mla_g_ckv[l], mla_w_ukv[l],
                         mla_g_q[l], mla_g_k[l], lru_conv_w[l], lru_conv_b[l], lru_w_r[l], lru_b_r[l],
                         lru_w_i[l], lru_b_i[l], lru_lam[l])
    return x


_drawn_inputs = setup_inputs


def setup_inputs(seed=0):
    import zlib

    import numpy as np

    out = dict(_drawn_inputs(seed))
    spreads = {}
    factors = {'gla_b_up': 8.0,
     'fox_g_q': 8.0,
     'fox_g_k': 7.983,
     'mla_g_cq': 8.0,
     'mla_g_ckv': 8.0,
     'mla_g_q': 8.0,
     'mla_g_k': 8.0,
     'lru_b_r': 8.0,
     'lru_b_i': 8.0}
    for name, (base, spread) in spreads.items():
        noise = np.random.default_rng([zlib.crc32(name.encode()), seed]).standard_normal(out[name].shape)
        drawn = base * np.exp(spread * noise) if base else spread * noise
        out[name] = __import__('jax').numpy.asarray(drawn.astype(out[name].dtype))
    for name, factor in factors.items():
        out[name] = (out[name] * factor).astype(out[name].dtype)
    return out
```

```python
from contextlib import ExitStack

import numpy as np

import concourse.bass as bass
from concourse import mybir

ALU = mybir.AluOpType
ACT = mybir.ActivationFunctionType
F32 = mybir.dt.float32
F32R = mybir.dt.float32r
BF16 = mybir.dt.bfloat16
I32 = mybir.dt.int32
AX_X = mybir.AxisListType.X

P = 128
BANK = 512
D_MODEL, SEQ, DEPTH = 1024, 1024, 2
KT = D_MODEL // P
TT = SEQ // P
D_MIX = 2 * D_MODEL
GROUP_W = D_MIX // 4
HEAD = 64
HEADS = GROUP_W // HEAD
HH = 4
HALF_W = HH * HEAD
CT = GROUP_W // P
EPS = 1e-6
DK, RANK = HEAD // 2, 16
GN = HEADS * DK // P
LEVELS = 7
Q_RANK, KV_RANK, ROPE = D_MODEL // 4, D_MODEL // 8, HEAD // 2
MLA_D = HEAD + ROPE
FOX_D = HEAD + 2
CONV_W, LRU_C = 4, 8.0
NEG = -1e30

IN_SIZES = (D_MIX, 256, 256, 512, RANK, 512, 512, 512, HEADS, Q_RANK, KV_RANK, ROPE, GROUP_W)
COL = np.concatenate([[0], np.cumsum(IN_SIZES)]).tolist()
(C_GATE, C_AQ, C_AK, C_AV, C_AG, C_BQ, C_BK, C_BV, C_BF, C_CQ, C_CKV, C_CKR, C_DX, D_IN) = COL
CHUNK = 256
CHUNK_MAX = CHUNK + RANK


class Trunk:

    def __init__(self, nc, dram, out, ctx):
        self.nc, self.dram, self.out, self.ctx = nc, dram, out, ctx
        self.sems, self.used = {}, {}
        self.x = self.sb(ctx, "x_res", [P, TT, D_MODEL])
        self.h_hi = self.sb(ctx, "h_hi", [P, KT, SEQ], F32R)
        self.h_lo = self.sb(ctx, "h_lo", [P, KT, SEQ], F32R)
        self.ident = self.sb(ctx, "ident", [P, P])
        self.ident_bf = self.sb(ctx, "ident_bf", [P, P], BF16)
        self.mask_bf = self.sb(ctx, "mask_bf", [P, P], BF16)
        self.cos = self.sb(ctx, "cos", [P, TT, ROPE // 2])
        self.sin = self.sb(ctx, "sin", [P, TT, ROPE // 2])
        self.psum = ctx.enter_context(nc.psum_tensor("psum", [P, 8, BANK], F32))

    def sb(self, ctx, name, shape, dt=F32):
        self.used[name] = self.used.get(name, 0) + 1
        name += f"_{self.used[name]}" if self.used[name] > 1 else ""
        return ctx.enter_context(self.nc.sbuf_tensor(name, shape, dt))

    def sem(self, name):
        if name not in self.sems:
            self.sems[name] = self.ctx.enter_context(self.nc.semaphore(name))
        return self.sems[name]

    def clear(self, names):
        with self.nc.Block() as block:
            @block.gpsimd
            def _(pool):
                for n in names:
                    pool.sem_clear(self.sems[n])


class Chain:

    def __init__(self, eng, sem):
        self.eng, self.sem, self.n = eng, sem, 0

    def __call__(self, ins):
        self.n += 1
        ins.then_inc(self.sem, 1)
        self.eng.wait_ge(self.sem, self.n)
        return ins


def bcast_rows(ap, n):
    return ap.rearrange("(a m) -> a m", a=1).to_broadcast([n, ap.shape[0]])


def head_bcast(ap, n):
    return ap.unsqueeze(2).to_broadcast([ap.shape[0], ap.shape[1], n])


def setup_block(k):
    nc, d = k.nc, k.dram
    HR = ROPE // 2
    loaded, step, stepped, act_step = (k.sem(n) for n in ("loaded", "dve_chain", "handover", "act_chain"))
    TWO_PI = 2.0 * np.pi
    C1 = float(np.float32(6.28125))
    C2 = 8116.0 / 2 ** 22
    C3 = float(np.float32(TWO_PI - C1 - C2))
    MAGIC = float(1.5 * 2 ** 23)
    with ExitStack() as s:
        pos_i = k.sb(s, "pos_i", [P, TT], I32)
        pos_f = k.sb(s, "pos_f", [P, TT])
        freq = k.sb(s, "freq", [P, HR])
        ang = k.sb(s, "ang", [P, TT, HR])
        turns = k.sb(s, "turns", [P, TT, HR])
        comp = k.sb(s, "comp", [P, TT, HR])
        with nc.Block() as block:
            @block.sync
            def _(sp):
                sp.dma_start(k.x[:, :, :], d["x"][0].rearrange("(t p) n -> p t n", p=P)).then_inc(loaded, 16)
                sp.dma_start(k.ident[:, :], d["c_ident"]).then_inc(loaded, 16)
                sp.dma_start(k.ident_bf[:, :], d["c_ident_bf"]).then_inc(loaded, 16)
                sp.dma_start(k.mask_bf[:, :], d["c_mask_bf"]).then_inc(loaded, 16)
                sp.dma_start(freq[:, :], d["c_freq"]).then_inc(loaded, 16)
                with nc.allow_non_contiguous_dma(reason="4 KB of positions"):
                    sp.dma_start(pos_i[:, :], d["positions"][0].rearrange("(t p) -> p t", p=P)).then_inc(loaded, 16)
                sp.wait_ge(loaded, 96)

            @block.vector
            def _(dve):
                link = Chain(dve, step)
                dve.wait_ge(loaded, 96)
                link(dve.tensor_copy(pos_f[:, :], pos_i[:, :]))
                link(dve.tensor_tensor(ang[:, :, :], head_bcast(pos_f[:, :], HR),
                                       freq[:, :].unsqueeze(1).to_broadcast([P, TT, HR]), ALU.mult))
                link(dve.tensor_scalar(turns[:, :, :], ang[:, :, :], 1.0 / TWO_PI, MAGIC, ALU.mult, ALU.add))
                link(dve.tensor_scalar(turns[:, :, :], turns[:, :, :], -MAGIC, None, ALU.add))
                for c in (C1, C2, C3):
                    link(dve.scalar_tensor_tensor(out=ang[:, :, :], in0=turns[:, :, :], scalar=-c, in1=ang[:, :, :],
                                                  op0=ALU.mult, op1=ALU.add))
                link(dve.tensor_scalar(ang[:, :, :], ang[:, :, :], 3.1415925, -3.1415925, ALU.min, ALU.max))
                link(dve.tensor_scalar(turns[:, :, :], ang[:, :, :], -1.0, None, ALU.mult))
                link(dve.tensor_tensor(comp[:, :, :], turns[:, :, :], ang[:, :, :], ALU.max))
                dve.tensor_scalar(comp[:, :, :], comp[:, :, :], -1.0, float(np.pi / 2), ALU.mult, ALU.add)\
                   .then_inc(stepped, 1)

            @block.scalar
            def _(act):
                act.wait_ge(stepped, 1)
                act.activation(k.sin[:, :, :], ang[:, :, :], ACT.Sin)
                act.activation(k.cos[:, :, :], comp[:, :, :], ACT.Sin).then_inc(act_step, 1)
                act.wait_ge(act_step, 1)
    k.clear(["loaded", "dve_chain", "handover", "act_chain"])


def norm_block(k, layer):
    nc, d = k.nc, k.dram
    names = ["loaded", "squares", "mean", "rstd", "act_chain", "normed", "transposed", "hi_done", "lo_done", "dve_chain"]
    loaded, squares, mean, rstd_ready, act_chain, normed, transposed, hi_done, lo_done, dve_chain = map(k.sem, names)
    with ExitStack() as s:
        gain = k.sb(s, "norm_gain", [P, D_MODEL])
        sq = k.sb(s, "norm_sq", [P, D_MODEL])
        ss = k.sb(s, "norm_ss", [P, TT])
        ms = k.sb(s, "norm_ms", [P, TT])
        rstd = k.sb(s, "norm_rstd", [P, TT])
        xn = k.sb(s, "norm_xn", [P, 2, D_MODEL])
        with nc.Block() as block:
            @block.sync
            def _(sp):
                sp.dma_start(gain[:, :], bcast_rows(d["norm_g"][layer], P)).then_inc(loaded, 16)

            @block.scalar
            def _(act):
                link = Chain(act, act_chain)
                for t in range(TT):
                    link(act.activation(sq[:, :], k.x[:, t, :], ACT.Square, accum_out=ss[:, t:t + 1]))
                act.sem_inc(squares, 1)
                act.wait_ge(mean, 1)
                link(act.activation(rstd[:, :], ms[:, :], ACT.Ln))
                act.activation(rstd[:, :], rstd[:, :], ACT.Exp, scale=-0.5).then_inc(rstd_ready, 1)
                for t in range(TT):
                    for j in range(2):
                        u = 2 * t + j
                        act.wait_ge(transposed, u + 1)
                        src = k.psum[:, u % 8, :].rearrange("p (c n) -> p c n", c=4)
                        act.activation(k.h_hi[:, 4 * j:4 * j + 4, t * P:(t + 1) * P], src, ACT.Copy)\
                           .then_inc(hi_done, 1)

            @block.vector
            def _(dve):
                link = Chain(dve, dve_chain)
                dve.wait_ge(squares, 1)
                dve.tensor_scalar(ms[:, :], ss[:, :], 1.0 / D_MODEL, EPS, ALU.mult, ALU.add).then_inc(mean, 1)
                dve.wait_ge(rstd_ready, 1)
                dve.wait_ge(loaded, 16)
                for t in range(TT + 1):
                    if t < TT:
                        if t >= 2:
                            dve.wait_ge(transposed, 2 * (t - 1))
                        dve.scalar_tensor_tensor(out=xn[:, t % 2, :], in0=k.x[:, t, :], scalar=rstd[:, t:t + 1],
                                                 in1=gain[:, :], op0=ALU.mult, op1=ALU.mult).then_inc(normed, 1)
                    if t >= 1:
                        for j in range(2):
                            u = 2 * (t - 1) + j
                            dve.wait_ge(hi_done, u + 1)
                            at = (slice(None), slice(4 * j, 4 * j + 4), slice((t - 1) * P, t * P))
                            src = k.psum[:, u % 8, :].rearrange("p (c n) -> p c n", c=4)
                            dve.tensor_tensor(k.h_lo[at], src, k.h_hi[at].bitcast(F32), ALU.subtract)\
                               .then_inc(lo_done, 1)

            @block.tensor
            def _(pe):
                for t in range(TT):
                    pe.wait_ge(normed, t + 1)
                    for j in range(2):
                        u = 2 * t + j
                        if u >= 8:
                            pe.wait_ge(lo_done, u - 7)
                        for c in range(4):
                            kk = 4 * j + c
                            last = pe.transpose(k.psum[:, u % 8, c * P:(c + 1) * P],
                                                xn[:, t % 2, kk * P:(kk + 1) * P], k.ident[:, :])
                        last.then_inc(transposed, 1)
    k.clear(names)


def project_block(k, layer, jobs, tag):
    nc, d = k.nc, k.dram
    names = ["w_landed0", "w_landed1", "w_hi", "w_lo", "unit_done", "act_evac", "dve_evac"]
    w_landed0, w_landed1, w_hi_ready, w_lo_ready, unit_done, act_evac, dve_evac = map(k.sem, names)
    w_landed = [w_landed0, w_landed1]
    w_in = d["w_in"][layer].rearrange("(k p) n -> p k n", p=P)
    units = []
    for j, (col, width, kind, evac) in enumerate(jobs):
        parts = [(m, n) for m in range(width // P) for n in range(SEQ // BANK)] if kind == "C" else range(TT)
        units += [(j, part) for part in parts]
    by = [jobs[j][3][0] for j, _ in units]
    nth = [by[:u + 1].count(by[u]) for u in range(len(units))]
    evac_sem = {"act": act_evac, "dve": dve_evac}
    with ExitStack() as s:
        raw = k.sb(s, tag + "_w_raw", [P, 2, KT, CHUNK_MAX])
        hi = k.sb(s, tag + "_w_hi", [P, 2, KT, CHUNK_MAX], F32R)
        lo = k.sb(s, tag + "_w_lo", [P, 2, KT, CHUNK_MAX], F32R)
        with nc.Block() as block:
            @block.sync
            def _(sp):
                for j, (col, width, kind, evac) in enumerate(jobs):
                    if j >= 2:
                        sp.wait_ge(w_lo_ready, j - 1)
                    sp.dma_start(raw[:, j % 2, :, :width], w_in[:, :, col:col + width]).then_inc(w_landed[j % 2], 16)

            def evacuate(eng, me, upto):
                for u in range(upto[0], upto[1]):
                    if by[u] != me:
                        continue
                    j, part = units[u]
                    eng.wait_ge(unit_done, u + 1)
                    jobs[j][3][1](eng, k.psum[:, u % 8, :], part).then_inc(evac_sem[me], 1)

            first_unit = [next(i for i, (jj, _) in enumerate(units) if jj == j) for j in range(len(jobs))]
            first_unit.append(len(units))

            @block.scalar
            def _(act):
                for j in range(len(jobs) + 2):
                    if j < len(jobs):
                        width = jobs[j][1]
                        act.wait_ge(w_landed[j % 2], 16 * (j // 2 + 1))
                        if j >= 2:
                            act.wait_ge(unit_done, first_unit[j - 1])
                        act.activation(hi[:, j % 2, :, :width], raw[:, j % 2, :, :width], ACT.Copy)\
                           .then_inc(w_hi_ready, 1)
                    if 1 <= j <= len(jobs):
                        evacuate(act, "act", (first_unit[j - 1], first_unit[j]))

            @block.gpsimd
            def _(pool):
                for j, (col, width, kind, evac) in enumerate(jobs):
                    pool.wait_ge(w_hi_ready, j + 1)
                    pool.tensor_tensor(lo[:, j % 2, :, :width], raw[:, j % 2, :, :width],
                                       hi[:, j % 2, :, :width].bitcast(F32), ALU.subtract).then_inc(w_lo_ready, 1)

            @block.vector
            def _(dve):
                evacuate(dve, "dve", (0, len(units)))

            @block.tensor
            def _(pe):
                for u, (j, part) in enumerate(units):
                    width, kind = jobs[j][1], jobs[j][2]
                    if u == first_unit[j]:
                        pe.wait_ge(w_lo_ready, j + 1)
                    if u >= 8:
                        pe.wait_ge(evac_sem[by[u - 8]], nth[u - 8])
                    for kk in range(KT):
                        for n, (w, h) in enumerate(((hi, k.h_hi), (hi, k.h_lo), (lo, k.h_hi))):
                            if kind == "C":
                                m, half = part
                                lhsT = w[:, j % 2, kk, m * P:(m + 1) * P]
                                rhs, o = h[:, kk, half * BANK:(half + 1) * BANK], k.psum[:, u % 8, :]
                            else:
                                lhsT, rhs = h[:, kk, part * P:(part + 1) * P], w[:, j % 2, kk, :width]
                                o = k.psum[:, u % 8, :width]
                            last = pe.matmul(o, lhsT, rhs, start=(kk == 0 and n == 0), stop=(kk == KT - 1 and n == 2))
                    last.then_inc(unit_done, 1)
    k.clear(names)


def w_out_rows(k, layer, mixer, part, tiles):
    r0 = mixer * GROUP_W + part * tiles * P
    return k.dram["w_out"][layer, r0:r0 + tiles * P, :].rearrange("(c p) n -> p c n", p=P)


def out_block(k, layer, mixer, y, tag):
    nc = k.nc
    names = ["w_landed", "w_hi", "w_lo", "y_hi", "y_lo", "unit_done", "added"]
    w_landed, w_hi_ready, w_lo_ready, y_hi_ready, y_lo_ready, unit_done, added = map(k.sem, names)
    NQ = D_MODEL // BANK
    units = [(n, t) for n in range(NQ) for t in range(TT)]
    with ExitStack() as s:
        w_raw = k.sb(s, tag + "_wo_raw", [P, CT, D_MODEL])
        w_hi = k.sb(s, tag + "_wo_hi", [P, CT, D_MODEL], F32R)
        w_lo = k.sb(s, tag + "_wo_lo", [P, CT, D_MODEL], F32R)
        y_hi = k.sb(s, tag + "_y_hi", [P, CT, SEQ], F32R)
        y_lo = k.sb(s, tag + "_y_lo", [P, CT, SEQ], F32R)

        def half(n):
            return slice(n * BANK, (n + 1) * BANK)

        with nc.Block() as block:
            @block.sync
            def _(sp):
                rows = w_out_rows(k, layer, mixer, 0, CT)
                for n in range(NQ):
                    if n >= 1:
                        sp.wait_ge(w_landed, 16 * n)
                    sp.dma_start(w_raw[:, :, half(n)], rows[:, :, half(n)]).then_inc(w_landed, 16)

            @block.scalar
            def _(act):
                for n in range(NQ):
                    act.activation(y_hi[:, :, half(n)], y[:, :, half(n)], ACT.Copy).then_inc(y_hi_ready, 1)
                for n in range(NQ):
                    act.wait_ge(w_landed, 16 * (n + 1))
                    act.activation(w_hi[:, :, half(n)], w_raw[:, :, half(n)], ACT.Copy).then_inc(w_hi_ready, 1)

            @block.gpsimd
            def _(pool):
                for n in range(NQ):
                    pool.wait_ge(w_hi_ready, n + 1)
                    pool.tensor_tensor(w_lo[:, :, half(n)], w_raw[:, :, half(n)], w_hi[:, :, half(n)].bitcast(F32),
                                       ALU.subtract).then_inc(w_lo_ready, 1)

            @block.vector
            def _(dve):
                for n in range(NQ):
                    dve.wait_ge(y_hi_ready, n + 1)
                    dve.tensor_tensor(y_lo[:, :, half(n)], y[:, :, half(n)], y_hi[:, :, half(n)].bitcast(F32),
                                      ALU.subtract).then_inc(y_lo_ready, 1)
                for u, (n, t) in enumerate(units):
                    dve.wait_ge(unit_done, u + 1)
                    at = k.x[:, t, half(n)]
                    dve.tensor_tensor(at, at, k.psum[:, u % 8, :], ALU.add).then_inc(added, 1)

            @block.tensor
            def _(pe):
                for u, (n, t) in enumerate(units):
                    if t == 0:
                        pe.wait_ge(w_lo_ready, n + 1)
                    if n == 0 and t % (TT // NQ) == 0:
                        pe.wait_ge(y_lo_ready, t // (TT // NQ) + 1)
                    if u >= 8:
                        pe.wait_ge(added, u - 7)
                    for c in range(CT):
                        for i, (a, b) in enumerate(((y_hi, w_hi), (y_hi, w_lo), (y_lo, w_hi))):
                            last = pe.matmul(k.psum[:, u % 8, :], a[:, c, t * P:(t + 1) * P], b[:, c, half(n)],
                                             start=(c == 0 and i == 0), stop=(c == CT - 1 and i == 2))
                    last.then_inc(unit_done, 1)
    k.clear(names)


def transpose_heads(pe, k, bank, src, width):
    for i in range(src.shape[1]):
        last = pe.transpose(k.psum[:width, bank, i * P:(i + 1) * P], src[:, i, :], k.ident[:, :])
    return last


def copy_evac(dst):
    return ("dve", lambda eng, ps, part: eng.tensor_copy(dst[part], ps[:, :dst[part].shape[-1]]))


def gate_jobs(sg, mixer, part, tiles):
    c0 = C_GATE + mixer * GROUP_W + part * tiles * P
    jobs = []
    for i in range(tiles * P // CHUNK):
        def evac(eng, ps, mn, i=i):
            m, n = mn
            return eng.activation(sg[:, 2 * i + m, n * BANK:(n + 1) * BANK], ps, ACT.Silu)
        jobs.append((c0 + i * CHUNK, CHUNK, "C", ("act", evac)))
    return jobs


def gla(k, layer):
    with ExitStack() as outer:
        sg = k.sb(outer, "gla_gate", [P, CT, SEQ])
        gla_inner(k, layer, sg)
        out_block(k, layer, 0, sg, "gla")


def gla_inner(k, layer, sg):
    with ExitStack() as s:
        qT = k.sb(s, "gla_qT", [P, GN, SEQ])
        kT = k.sb(s, "gla_kT", [P, GN, SEQ])
        v = k.sb(s, "gla_v", [P, TT, GROUP_W])
        a_tok = k.sb(s, "gla_a", [P, TT, RANK])

        def c_copy(dst):
            return ("dve", lambda eng, ps, mn: eng.tensor_copy(dst[:, mn[0], mn[1] * BANK:(mn[1] + 1) * BANK], ps))

        def q_copy(eng, ps, mn):
            return eng.tensor_scalar(qT[:, mn[0], mn[1] * BANK:(mn[1] + 1) * BANK], ps, DK ** -0.5, None, ALU.mult)

        def v_copy(eng, ps, t):
            return eng.tensor_copy(v[:, t, 0:CHUNK], ps[:, :CHUNK])

        def v2_copy(eng, ps, t):
            return eng.tensor_copy(v[:, t, CHUNK:], ps[:, :CHUNK])

        def a_copy(eng, ps, t):
            return eng.tensor_copy(a_tok[:, t, :], ps[:, :RANK])

        project_block(k, layer, [
            (C_AQ, CHUNK, "C", ("dve", q_copy)), (C_AK, CHUNK, "C", c_copy(kT)),
            (C_AV, CHUNK, "T", ("dve", v_copy)), (C_AV + CHUNK, CHUNK, "T", ("dve", v2_copy)),
            (C_AG, RANK, "T", ("dve", a_copy)),
        ] + gate_jobs(sg, 0, 0, CT), "gla")

        G = k.sb(s, "gla_G", [P, GN, SEQ])
        gla_decay_block(k, layer, s, a_tok, G)
        gla_mix_block(k, layer, qT, kT, v, sg, G)


def gla_decay_block(k, layer, s, a_tok, G):
    nc, d = k.nc, k.dram
    names = ["loaded", "transposed", "copied", "product", "biased", "logs", "act_chain", "summed"]
    loaded, transposed, copied, product, biased, logs, act_chain, summed = map(k.sem, names)
    N16 = SEQ // BANK
    with ExitStack() as s2:
        w_up = k.sb(s2, "gla_w_up", [RANK, GN * P])
        b_up = k.sb(s2, "gla_b_up", [P, GN])
        aT = k.sb(s2, "gla_aT", [RANK, SEQ])
        z = k.sb(s2, "gla_z", [P, GN, SEQ])
        e = k.sb(s2, "gla_e", [P, GN, SEQ])
        ls = k.sb(s2, "gla_ls", [P, GN, SEQ])
        ones = k.sb(s2, "gla_ones", [P, P])
        with nc.Block() as block:
            @block.sync
            def _(sp):
                sp.dma_start(w_up[:, :], d["gla_w_up"][layer]).then_inc(loaded, 16)
                with nc.allow_non_contiguous_dma(reason="256 biases"):
                    sp.dma_start(b_up[:, :], d["gla_b_up"][layer].rearrange("(g p) -> p g", p=P)).then_inc(loaded, 16)

            @block.tensor
            def _(pe):
                for t in range(TT):
                    last = pe.transpose(k.psum[:RANK, t // 4, (t % 4) * P:(t % 4 + 1) * P], a_tok[:, t, :], k.ident[:, :])
                    if t % 4 == 3:
                        last.then_inc(transposed, 1)
                pe.wait_ge(loaded, 32)
                for g in range(GN):
                    for n in range(N16):
                        pe.wait_ge(copied, n + 1)
                        pe.matmul(k.psum[:, 2 + g * N16 + n, :], w_up[:, g * P:(g + 1) * P],
                                  aT[:, n * BANK:(n + 1) * BANK], start=True, stop=True).then_inc(product, 1)

            @block.vector
            def _(dve):
                dve.memset(ones[:, :], 1.0)
                for n in range(N16):
                    dve.wait_ge(transposed, n + 1)
                    dve.tensor_copy(aT[:, n * BANK:(n + 1) * BANK], k.psum[:RANK, n, :]).then_inc(copied, 1)
                dve.wait_ge(loaded, 32)
                for g in range(GN):
                    for n in range(N16):
                        dve.wait_ge(product, g * N16 + n + 1)
                        dve.tensor_scalar(z[:, g, n * BANK:(n + 1) * BANK], k.psum[:, 2 + g * N16 + n, :],
                                          b_up[:, g:g + 1], None, ALU.add).then_inc(biased, 1)
                dve.wait_ge(logs, 1)
                dve.scalar_tensor_tensor(out=ls[:, :, :], in0=z[:, :, :], scalar=0.0, in1=e[:, :, :],
                                         op0=ALU.min, op1=ALU.subtract).then_inc(summed, 1)
                dve.wait_ge(summed, 1)
                for g in range(GN):
                    for t in range(TT):
                        dve.tensor_tensor_scan(G[:, g, t * P:(t + 1) * P], ones[:, :], ls[:, g, t * P:(t + 1) * P],
                                               0.0, ALU.mult, ALU.add).then_inc(summed, 1)
                dve.wait_ge(summed, 1 + GN * TT)

            @block.scalar
            def _(act):
                link = Chain(act, act_chain)
                act.wait_ge(biased, GN * N16)
                link(act.activation(e[:, :, :], z[:, :, :], ACT.Abs))
                link(act.activation(e[:, :, :], e[:, :, :], ACT.Exp, scale=-1.0))
                act.activation(e[:, :, :], e[:, :, :], ACT.Ln, bias=1.0).then_inc(logs, 1)
    k.clear(names)


def gla_mix_block(k, layer, qT, kT, v, sg, G):
    nc, d = k.nc, k.dram
    names = ["loaded", "exponents", "decays", "q_expanded", "q_level", "k_level", "level_done", "masked",
             "chunk_ends", "k_end_turned", "k_end_copied", "out_done", "state_product", "state_new", "squares",
             "mean", "rstd", "normed", "y_turned", "y_ready", "dve_chain", "act_chain"]
    (loaded, exponents, decays, q_expanded, q_level, k_level, level_done, masked, chunk_ends, k_end_turned,
     k_end_copied, out_done, state_product, state_new, squares, mean, rstd_ready, normed, y_turned, y_ready,
     dve_chain, act_chain) = map(k.sem, names)
    NL = LEVELS + 1
    UN = TT * GN
    IN, END = LEVELS, LEVELS + 1
    NB, B_OUT, B_STATE, B_KT, B_Y = 4, 4, 5, 6, 7
    QR, KR, AR = 3, 4, 4
    with ExitStack() as s:
        g_out = k.sb(s, "gla_g_out", [P, 1])
        masks = k.sb(s, "gla_masks", [P, LEVELS, P], I32)
        head_mask = k.sb(s, "gla_head_mask", [P, HH])
        E = k.sb(s, "gla_E", [P, 2, LEVELS + 2, GN, P])
        q4 = k.sb(s, "gla_q4", [P, 2, HH, P])
        ql = k.sb(s, "gla_ql", [P, QR, HH, P])
        kl = k.sb(s, "gla_kl", [P, KR, P])
        q_s = k.sb(s, "gla_q_start", [P, GN, P])
        k_e = k.sb(s, "gla_k_end", [P, GN, P])
        k_et = k.sb(s, "gla_k_end_tok", [P, GN * P])
        A = k.sb(s, "gla_A", [P, AR, HH, P])
        S = k.sb(s, "gla_S", [P, GN, HH, HEAD])
        sq = k.sb(s, "gla_sq", [P, GROUP_W])
        ms = k.sb(s, "gla_ms", [P, HEADS])
        rstd = k.sb(s, "gla_rstd", [P, HEADS])
        on = k.sb(s, "gla_on", [P, GROUP_W])

        def tok(c):
            return slice(c * P, (c + 1) * P)

        with nc.Block() as block:
            @block.sync
            def _(sp):
                sp.dma_start(masks[:, :, :], d["c_masks"]).then_inc(loaded, 16)
                sp.dma_start(head_mask[:, :], d["c_head_mask"]).then_inc(loaded, 16)
                with nc.allow_non_contiguous_dma(reason="64 gains"):
                    for i in range(P // HEAD):
                        sp.dma_start(g_out[i * HEAD:(i + 1) * HEAD, :],
                                     d["gla_g_out"][layer].rearrange("(p a) -> p a", a=1)).then_inc(loaded, 16)

            @block.gpsimd
            def _(pool):
                pool.wait_ge(loaded, 64)
                for u in range(UN):
                    c, g = u // GN, u % GN
                    if u >= 2:
                        pool.wait_ge(q_level, LEVELS * (u - 1))
                        pool.wait_ge(level_done, NL * (u - 2) + 1)
                    pool.tensor_tensor(q4[:, u % 2, :, :], qT[:, g, tok(c)].unsqueeze(1).to_broadcast([P, HH, P]),
                                       head_bcast(head_mask[:, :], P), ALU.mult).then_inc(q_expanded, 1)
                    if g == 0:
                        pool.wait_ge(decays, c + 1)
                    for j in range(1, NL):
                        m = LEVELS * u + j - 1
                        if m >= KR:
                            before = m - KR
                            pool.wait_ge(level_done, NL * (before // LEVELS) + before % LEVELS + 2)
                        pool.tensor_tensor(kl[:, m % KR, :], kT[:, g, tok(c)], E[:, c % 2, j - 1, g, :], ALU.mult)\
                            .then_inc(k_level, 1)
                    if g == GN - 1:
                        if c >= 1:
                            pool.wait_ge(out_done, c)
                            pool.wait_ge(k_end_turned, c)
                        pool.tensor_tensor(q_s[:, :, :], qT[:, :, tok(c)], E[:, c % 2, IN, :, :], ALU.mult)
                        pool.tensor_tensor(k_e[:, :, :], kT[:, :, tok(c)], E[:, c % 2, END, :, :], ALU.mult)\
                            .then_inc(chunk_ends, 1)

            @block.vector
            def _(dve):
                link = Chain(dve, dve_chain)
                dve.memset(S[:, :, :, :], 0.0).then_inc(state_new, 1)
                dve.wait_ge(state_new, 1)
                dve.wait_ge(loaded, 64)

                def chunk_exponents(c):
                    if c >= 2:
                        dve.wait_ge(k_level, LEVELS * GN * (c - 1))
                        dve.wait_ge(chunk_ends, c - 1)
                        dve.wait_ge(q_level, LEVELS * GN * (c - 1))
                        dve.wait_ge(state_new, c)
                    for j in range(LEVELS):
                        B = 64 >> j
                        for g in range(GN):
                            gv = G[:, g, tok(c)].rearrange("p (n h b) -> p n h b", h=2, b=B)
                            ev = E[:, c % 2, j, g, :].rearrange("p (n h b) -> p n h b", h=2, b=B)
                            edge = gv[:, :, 0, B - 1:B].to_broadcast([P, 64 // B, B])
                            dve.tensor_tensor(ev[:, :, 1, :], gv[:, :, 1, :], edge, ALU.subtract)
                            dve.tensor_tensor(ev[:, :, 0, :], edge, gv[:, :, 0, :], ALU.subtract)
                    dve.tensor_copy(E[:, c % 2, IN, :, :], G[:, :, tok(c)])
                    end = G[:, :, (c + 1) * P - 1:(c + 1) * P].to_broadcast([P, GN, P])
                    dve.tensor_tensor(E[:, c % 2, END, :, :], end, G[:, :, tok(c)], ALU.subtract).then_inc(exponents, 1)

                def mask(n):
                    u, j = n // NL, n % NL
                    dve.wait_ge(level_done, n + 1)
                    ps = k.psum[:, n % NB, :].rearrange("p (h t) -> p h t", h=HH)
                    if j == 0:
                        if u >= AR:
                            dve.wait_ge(out_done, (u - AR) // GN + 1)
                        m = k.ident[:, :].unsqueeze(1).to_broadcast([P, HH, P])
                        dve.tensor_tensor(A[:, u % AR, :, :], ps, m, ALU.mult).then_inc(masked, 1)
                    else:
                        dve.wait_ge(masked, n)
                        m = masks[:, j - 1, :].unsqueeze(1).to_broadcast([P, HH, P])
                        dve.copy_predicated(A[:, u % AR, :, :], m, ps).then_inc(masked, 1)

                def levels(u):
                    c, g = u // GN, u % GN
                    for j in range(NL):
                        n = NL * u + j
                        if j >= 1:
                            m = LEVELS * u + j - 1
                            if j == 1:
                                dve.wait_ge(q_expanded, u + 1)
                                dve.wait_ge(decays, c + 1)
                            if m >= QR:
                                before = m - QR
                                dve.wait_ge(level_done, NL * (before // LEVELS) + before % LEVELS + 2)
                            e = E[:, c % 2, j - 1, g, :].unsqueeze(1).to_broadcast([P, HH, P])
                            dve.tensor_tensor(ql[:, m % QR, :, :], q4[:, u % 2, :, :], e, ALU.mult).then_inc(q_level, 1)
                        if n >= 2:
                            mask(n - 2)

                def y_evac(c):
                    dve.wait_ge(y_turned, c + 1)
                    at = sg[:, :, tok(c)]
                    dve.scalar_tensor_tensor(out=at, in0=k.psum[:, B_Y, :].rearrange("p (c n) -> p c n", c=CT),
                                             scalar=g_out[:, 0:1], in1=at, op0=ALU.mult, op1=ALU.mult)\
                       .then_inc(y_ready, 1)

                def state(c):
                    dve.wait_ge(state_product, c + 1)
                    for g in range(GN):
                        for i in range(HH):
                            r = slice(DK * i, DK * (i + 1))
                            col = g * HALF_W + i * HEAD
                            last = dve.scalar_tensor_tensor(
                                out=S[r, g, i, :], in0=S[r, g, i, :], scalar=E[r, c % 2, IN, g, P - 1:P],
                                in1=k.psum[r, B_STATE, col:col + HEAD], op0=ALU.mult, op1=ALU.add)
                    last.then_inc(state_new, 1)

                def means(c):
                    dve.wait_ge(squares, c + 1)
                    link(dve.tensor_reduce(ms[:, :], sq[:, :].rearrange("p (h e) -> p h e", e=HEAD), AX_X, ALU.add))
                    dve.tensor_scalar(ms[:, :], ms[:, :], 1.0 / HEAD, EPS, ALU.mult, ALU.add).then_inc(mean, 1)

                def normalise(c):
                    dve.wait_ge(rstd_ready, c + 1)
                    if c >= 1:
                        dve.wait_ge(y_turned, c)
                    dve.tensor_tensor(on[:, :].rearrange("p (h e) -> p h e", e=HEAD),
                                      k.psum[:, B_OUT, :].rearrange("p (h e) -> p h e", e=HEAD),
                                      head_bcast(rstd[:, :], HEAD), ALU.mult).then_inc(normed, 1)

                chunk_exponents(0)
                for c in range(TT + 1):
                    if c < TT:
                        levels(GN * c)
                    else:
                        mask(NL * UN - 2)
                        mask(NL * UN - 1)
                    if c >= 2:
                        y_evac(c - 2)
                    if 1 <= c < TT:
                        state(c - 1)
                    if c + 1 < TT:
                        chunk_exponents(c + 1)
                    if c >= 1:
                        means(c - 1)
                    if c < TT:
                        levels(GN * c + 1)
                    if c >= 1:
                        normalise(c - 1)
                y_evac(TT - 1)

            @block.scalar
            def _(act):
                link = Chain(act, act_chain)

                def decay(c):
                    act.wait_ge(exponents, c + 1)
                    at = E[:, c % 2, :, :, :]
                    act.activation(at, at, ACT.Exp, scale=1.0 / 16.0).then_inc(decays, 1)

                decay(0)
                for c in range(TT + 1):
                    if c >= 1:
                        act.wait_ge(k_end_turned, c)
                        act.activation(k_et[:, :], k.psum[:, B_KT, :GN * P], ACT.Copy).then_inc(k_end_copied, 1)
                        act.wait_ge(out_done, c)
                        act.activation(sq[:, :], k.psum[:, B_OUT, :], ACT.Square).then_inc(squares, 1)
                    if c + 1 < TT:
                        decay(c + 1)
                    if c >= 1:
                        act.wait_ge(mean, c)
                        link(act.activation(rstd[:, :], ms[:, :], ACT.Ln))
                        act.activation(rstd[:, :], rstd[:, :], ACT.Exp, scale=-0.5).then_inc(rstd_ready, 1)

            @block.tensor
            def _(pe):
                def levels(u):
                    c, g = u // GN, u % GN
                    for j in range(NL):
                        n = NL * u + j
                        if n >= NB:
                            pe.wait_ge(masked, n - NB + 1)
                        if j == 0:
                            pe.wait_ge(q_expanded, u + 1)
                            lhsT, rhs = kT[:, g, tok(c)], q4[:, u % 2, :, :]
                        else:
                            m = LEVELS * u + j - 1
                            pe.wait_ge(q_level, m + 1)
                            pe.wait_ge(k_level, m + 1)
                            lhsT, rhs = kl[:, m % KR, :], ql[:, m % QR, :, :]
                        pe.matmul(k.psum[:, n % NB, :], lhsT, rhs.rearrange("p h t -> p (h t)"), start=True, stop=True)\
                          .then_inc(level_done, 1)

                def finish(c):
                    pe.wait_ge(chunk_ends, c + 1)
                    if c >= 1:
                        pe.wait_ge(k_end_copied, c)
                        pe.wait_ge(normed, c)
                    for g in range(GN):
                        last = pe.transpose(k.psum[:, B_KT, g * P:(g + 1) * P], k_e[:, g, :], k.ident[:, :])
                    last.then_inc(k_end_turned, 1)
                    pe.wait_ge(masked, NL * GN * (c + 1))
                    pe.wait_ge(state_new, c + 1)
                    for g in range(GN):
                        o = k.psum[:, B_OUT, g * HALF_W:(g + 1) * HALF_W]
                        pe.matmul(o, q_s[:, g, :], S[:, g, :, :].rearrange("p h e -> p (h e)"), start=True, stop=False,
                                  skip_group_check=True)
                        for i in range(HH):
                            last = pe.matmul(o[:, i * HEAD:(i + 1) * HEAD], A[:, (GN * c + g) % AR, i, :],
                                             v[:, c, g * HALF_W + i * HEAD:g * HALF_W + (i + 1) * HEAD],
                                             start=False, stop=(i == HH - 1), skip_group_check=True)
                    last.then_inc(out_done, 1)
                    if c < TT - 1:
                        pe.wait_ge(k_end_copied, c + 1)
                        for g in range(GN):
                            last = pe.matmul(k.psum[:, B_STATE, g * HALF_W:(g + 1) * HALF_W], k_et[:, g * P:(g + 1) * P],
                                             v[:, c, g * HALF_W:(g + 1) * HALF_W], start=True, stop=True)
                        last.then_inc(state_product, 1)

                def turn_y(c):
                    pe.wait_ge(normed, c + 1)
                    if c >= 1:
                        pe.wait_ge(y_ready, c)
                    for i in range(CT):
                        last = pe.transpose(k.psum[:, B_Y, i * P:(i + 1) * P], on[:, i * P:(i + 1) * P], k.ident[:, :])
                    last.then_inc(y_turned, 1)

                pe.wait_ge(loaded, 64)
                for c in range(TT + 1):
                    if c < TT:
                        levels(GN * c)
                    if c >= 1:
                        finish(c - 1)
                    if c < TT:
                        levels(GN * c + 1)
                    if c >= 1:
                        turn_y(c - 1)
    k.clear(names)


def turn_block(k, q, kk, qT, kT, q_gain, k_gain, width):
    nc = k.nc
    names = ["q_turned", "k_turned", "q_evac", "k_evac"]
    q_turned, k_turned, q_evac, k_evac = map(k.sem, names)
    RING = 4
    with nc.Block() as block:
        @block.tensor
        def _(pe):
            for t in range(TT):
                for src, bank, turned, evac in ((q, 0, q_turned, q_evac), (kk, RING, k_turned, k_evac)):
                    if t >= RING:
                        pe.wait_ge(evac, t - RING + 1)
                    for h in range(HH):
                        last = pe.transpose(k.psum[:width, bank + t % RING, h * P:(h + 1) * P], src[:, t, h, :],
                                            k.ident[:, :])
                    last.then_inc(turned, 1)

        @block.scalar
        def _(act):
            for t in range(TT):
                act.wait_ge(q_turned, t + 1)
                src = k.psum[:width, t % RING, :].rearrange("p (h n) -> p h n", h=HH)
                act.activation(qT[:, :, t * P:(t + 1) * P], src, ACT.Copy, scale=q_gain[:, 0:1]).then_inc(q_evac, 1)

        @block.vector
        def _(dve):
            for t in range(TT):
                dve.wait_ge(k_turned, t + 1)
                src = k.psum[:width, RING + t % RING, :].rearrange("p (h n) -> p h n", h=HH)
                dve.tensor_scalar(kT[:, :, t * P:(t + 1) * P], src, k_gain[:, 0:1], None, ALU.mult)\
                   .then_inc(k_evac, 1)
    k.clear(names)


def attention_block(k, qT, kT, v, sg, p_buf, pt_buf, tag):
    nc = k.nc
    names = ["scores", "max_done", "probs", "p_turned", "pt_dve", "pt_act", "pv_done", "normed", "y_turned",
             "y_ready", "dve_chain"]
    (scores, max_done, probs, p_turned, pt_dve, pt_act, pv_done, normed, y_turned, y_ready,
     dve_chain) = map(k.sem, names)
    U = TT * HH
    B_PT, B_O, GROUP = 4, 6, 4
    groups = [(u, g) for u in range(U) for g in range((u // HH) // GROUP + 1)]
    first = {u: groups.index((u, 0)) for u in range(U)}
    by = ["act" if g % 2 else "dve" for _, g in groups]
    nth = [by[:i + 1].count(by[i]) for i in range(len(groups))]
    pt_sem = {"dve": pt_dve, "act": pt_act}

    def blocks(u, g):
        return range(g * GROUP, min((g + 1) * GROUP, u // HH + 1))

    def group_list(u):
        return [(first[u] + g, blocks(u, g)) for g in range((u // HH) // GROUP + 1)]

    def score_ap(u):
        b = 2 * (u % 2)
        return k.psum[:, b:b + 2, :].rearrange("p b n -> p (b n)")[:, :(u // HH + 1) * P]

    with ExitStack() as s:
        nmax = k.sb(s, tag + "_nmax", [P, U])
        rsum = k.sb(s, tag + "_rsum", [P, U])
        rinv = k.sb(s, tag + "_rinv", [P, U])
        on = k.sb(s, tag + "_on", [P, HALF_W])
        p_sb = p_buf[:, :2 * SEQ].rearrange("p (a n) -> p a n", a=2)
        pt_sb = pt_buf[:, :2 * SEQ].rearrange("p (a n) -> p a n", a=2)

        def copy_pt(eng, me, u, op):
            for i, bl in group_list(u):
                if by[i] == me:
                    eng.wait_ge(p_turned, i + 1)
                    if u >= 2:
                        eng.wait_ge(pv_done, u - 1)
                    op(pt_sb[:, u % 2, bl[0] * P:(bl[-1] + 1) * P], k.psum[:, B_PT + i % 2, :len(bl) * P])\
                        .then_inc(pt_sem[me], 1)

        with nc.Block() as block:
            @block.tensor
            def _(pe):
                def score(u):
                    qt, h = u // HH, u % HH
                    if u >= 2:
                        pe.wait_ge(probs, u - 1)
                    out, n = score_ap(u), (qt + 1) * P
                    for c0 in range(0, n, BANK):
                        c1 = min(c0 + BANK, n)
                        pe.matmul(out[:, c0:c1], qT[:, h, qt * P:(qt + 1) * P], kT[:, h, c0:c1], start=True,
                                  stop=(c1 < n))
                    pe.matmul(out[:, qt * P:n], k.ident_bf[:, :], k.mask_bf[:, :], start=False, stop=True)\
                      .then_inc(scores, 1)

                def turn(u):
                    pe.wait_ge(probs, u + 1)
                    for i, bl in group_list(u):
                        if i >= 2:
                            pe.wait_ge(pt_sem[by[i - 2]], nth[i - 2])
                        for j, b in enumerate(bl):
                            last = pe.transpose(k.psum[:, B_PT + i % 2, j * P:(j + 1) * P],
                                                p_sb[:, u % 2, b * P:(b + 1) * P], k.ident[:, :])
                        last.then_inc(p_turned, 1)

                def pv(u):
                    qt, h = u // HH, u % HH
                    if h == 0 and qt >= 2:
                        pe.wait_ge(y_ready, qt - 1)
                    for i, bl in group_list(u):
                        pe.wait_ge(pt_sem[by[i]], nth[i])
                        for b in bl:
                            last = pe.matmul(k.psum[:, B_O + qt % 2, h * HEAD:(h + 1) * HEAD],
                                             pt_sb[:, u % 2, b * P:(b + 1) * P], v[:, b, h * HEAD:(h + 1) * HEAD],
                                             start=(b == 0), stop=(b == qt))
                    last.then_inc(pv_done, 1)

                def turn_y(qt):
                    pe.wait_ge(normed, qt + 1)
                    for i in range(HALF_W // P):
                        last = pe.transpose(k.psum[:, B_O + qt % 2, HALF_W + i * P:HALF_W + (i + 1) * P],
                                            on[:, i * P:(i + 1) * P], k.ident[:, :])
                    last.then_inc(y_turned, 1)

                for u in range(U + 2):
                    if u < U:
                        score(u)
                    if 1 <= u <= U:
                        turn(u - 1)
                    if u >= 2:
                        pv(u - 2)
                        if (u - 2) % HH == 1 and u - 2 > HH:
                            turn_y((u - 2) // HH - 1)
                turn_y(TT - 1)

            @block.vector
            def _(dve):
                link = Chain(dve, dve_chain)

                def normalise(qt):
                    dve.wait_ge(pv_done, HH * (qt + 1))
                    if qt >= 1:
                        dve.wait_ge(y_turned, qt)
                    cols = slice(HH * qt, HH * (qt + 1))
                    link(dve.reciprocal(rinv[:, cols], rsum[:, cols]))
                    dve.tensor_tensor(on[:, :].rearrange("p (h e) -> p h e", e=HEAD),
                                      k.psum[:, B_O + qt % 2, :HALF_W].rearrange("p (h e) -> p h e", e=HEAD),
                                      head_bcast(rinv[:, cols], HEAD), ALU.mult).then_inc(normed, 1)

                def y_evac(qt):
                    dve.wait_ge(y_turned, qt + 1)
                    at = sg[:, :, qt * P:(qt + 1) * P]
                    dve.tensor_tensor(at, k.psum[:, B_O + qt % 2, HALF_W:].rearrange("p (c n) -> p c n", n=P), at,
                                      ALU.mult).then_inc(y_ready, 1)

                for u in range(U + 1):
                    if u < U:
                        dve.wait_ge(scores, u + 1)
                        dve.tensor_reduce(nmax[:, u:u + 1], score_ap(u), AX_X, ALU.max, negate=True)\
                           .then_inc(max_done, 1)
                    if u >= 1:
                        copy_pt(dve, "dve", u - 1, dve.tensor_copy)
                    if u % HH == 2 and u > HH:
                        normalise(u // HH - 1)
                    if u % HH == 3 and u > HH:
                        y_evac(u // HH - 1)
                normalise(TT - 1)
                y_evac(TT - 1)

            @block.scalar
            def _(act):
                for u in range(U + 1):
                    if u < U:
                        act.wait_ge(max_done, u + 1)
                        if u >= 2:
                            act.wait_ge(p_turned, first[u - 1])
                        n = (u // HH + 1) * P
                        act.activation(p_sb[:, u % 2, :n], score_ap(u), ACT.Exp, bias=nmax[:, u:u + 1],
                                       accum_out=rsum[:, u:u + 1]).then_inc(probs, 1)
                    if u >= 1:
                        copy_pt(act, "act", u - 1, lambda o, i: act.activation(o, i, ACT.Copy))
    k.clear(names)


def fox(k, layer):
    nc, d = k.nc, k.dram
    with ExitStack() as s:
        sg = k.sb(s, "fox_gate", [P, CT, SEQ])
        cum = k.sb(s, "fox_cum", [P, 2, TT, HEADS])
        f_tok = k.sb(s, "fox_f", [P, TT, HEADS])
        q_gain = k.sb(s, "fox_q_gain", [FOX_D, 1])
        k_gain = k.sb(s, "fox_k_gain", [FOX_D, 1])
        for half in (1, 0):
            with ExitStack() as s2:
                v = k.sb(s2, "fox_v", [P, TT, HALF_W])
                q_raw = k.sb(s2, "fox_q", [P, TT, HALF_W])
                k_raw = k.sb(s2, "fox_k", [P, TT, HALF_W])

                def to(dst):
                    return ("dve", lambda eng, ps, t: eng.tensor_copy(dst[:, t, :], ps[:, :HALF_W]))

                def v_and_f(eng, ps, t):
                    eng.tensor_copy(v[:, t, :], ps[:, :HALF_W])
                    return eng.tensor_copy(f_tok[:, t, :], ps[:, HALF_W:HALF_W + HEADS])

                off = half * HALF_W
                jobs = [(C_BQ + off, HALF_W, "T", to(q_raw)), (C_BK + off, HALF_W, "T", to(k_raw))]
                if half == 1:
                    jobs += [(C_BV + off, HALF_W + HEADS, "T", ("dve", v_and_f))] + gate_jobs(sg, 1, 0, CT)
                else:
                    jobs += [(C_BV + off, HALF_W, "T", to(v))]
                project_block(k, layer, jobs, "fox")
                if half == 1:
                    forget_block(k, layer, f_tok, cum, q_gain, k_gain)
                with ExitStack() as s3:
                    qT = k.sb(s3, "fox_qT", [FOX_D, HH, SEQ])
                    kT = k.sb(s3, "fox_kT", [FOX_D, HH, SEQ])
                    with ExitStack() as s4:
                        qa = k.sb(s4, "fox_qa", [P, TT, HH, FOX_D])
                        ka = k.sb(s4, "fox_ka", [P, TT, HH, FOX_D])
                        fox_norm_block(k, s4, q_raw, k_raw, qa, ka, cum, half)
                        turn_block(k, qa, ka, qT, kT, q_gain, k_gain, FOX_D)
                    attention_block(k, qT, kT, v, sg[:, 2 * half:2 * half + 2, :],
                                    q_raw[:, :, :].rearrange("p t n -> p (t n)"),
                                    k_raw[:, :, :].rearrange("p t n -> p (t n)"), "fox")
        out_block(k, layer, 1, sg, "fox")


def forget_block(k, layer, f_tok, cum, q_gain, k_gain):
    nc, d = k.nc, k.dram
    names = ["loaded", "dve_chain", "handover", "logs", "act_chain", "product"]
    loaded, dve_chain, handover, logs, act_chain, product = map(k.sem, names)
    with ExitStack() as s:
        bias = k.sb(s, "fox_b", [P, HEADS])
        upper = k.sb(s, "fox_upper", [P, P])
        ones = k.sb(s, "fox_ones", [P, P])
        z = k.sb(s, "fox_z", [P, TT, HEADS])
        az = k.sb(s, "fox_az", [P, TT, HEADS])
        ls = k.sb(s, "fox_ls", [P, TT, HEADS])
        before = k.sb(s, "fox_before", [P, TT, HEADS])
        flat = "p t h -> p (t h)"
        with nc.Block() as block:
            @block.sync
            def _(sp):
                sp.dma_start(bias[:, :], bcast_rows(d["fox_b_f"][layer], P)).then_inc(loaded, 16)
                sp.dma_start(upper[:, :], d["c_upper"]).then_inc(loaded, 16)
                for g, name in ((q_gain, "fox_g_q"), (k_gain, "fox_g_k")):
                    with nc.allow_non_contiguous_dma(reason="64 gains"):
                        sp.dma_start(g[:HEAD, :], d[name][layer].rearrange("(p a) -> p a", a=1)).then_inc(loaded, 16)

            @block.vector
            def _(dve):
                link = Chain(dve, dve_chain)
                dve.memset(q_gain[HEAD:FOX_D, :], 1.0)
                dve.memset(k_gain[HEAD:FOX_D, :], 1.0)
                dve.memset(ones[:, :], 1.0)
                dve.wait_ge(loaded, 64)
                dve.tensor_scalar(q_gain[:HEAD, :], q_gain[:HEAD, :], HEAD ** -0.5, None, ALU.mult)
                link(dve.tensor_tensor(z[:, :, :], f_tok[:, :, :], bias[:, :].unsqueeze(1).to_broadcast([P, TT, HEADS]),
                                       ALU.add))
                link(dve.tensor_scalar(az[:, :, :], z[:, :, :], -1.0, None, ALU.mult))
                dve.tensor_tensor(az[:, :, :], az[:, :, :], z[:, :, :], ALU.max).then_inc(handover, 1)
                dve.wait_ge(logs, 1)
                link(dve.scalar_tensor_tensor(out=ls[:, :, :], in0=z[:, :, :], scalar=0.0, in1=az[:, :, :],
                                              op0=ALU.min, op1=ALU.subtract))
                link(dve.memset(before[:, 0, :], 0.0))
                for t in range(1, TT):
                    link(dve.tensor_tensor(before[:, t, :], before[:, t - 1, :], ls[:, t - 1, :], ALU.add))
                dve.sem_inc(handover, 1)
                dve.wait_ge(product, 1)
                dve.tensor_copy(cum[:, 0, :, :].rearrange(flat), k.psum[:, 0, :TT * HEADS])
                link(dve.tensor_scalar(cum[:, 1, :, :].rearrange(flat), k.psum[:, 0, :TT * HEADS], -1.0, None, ALU.mult))

            @block.scalar
            def _(act):
                link = Chain(act, act_chain)
                act.wait_ge(handover, 1)
                link(act.activation(az[:, :, :], az[:, :, :], ACT.Exp, scale=-1.0))
                act.activation(az[:, :, :], az[:, :, :], ACT.Ln, bias=1.0).then_inc(logs, 1)

            @block.tensor
            def _(pe):
                pe.wait_ge(handover, 2)
                pe.matmul(k.psum[:, 0, :TT * HEADS], upper[:, :], ls[:, :, :].rearrange(flat), start=True, stop=False)
                pe.matmul(k.psum[:, 0, :TT * HEADS], ones[:, :], before[:, :, :].rearrange(flat), start=False,
                          stop=True).then_inc(product, 1)
    k.clear(names)


def fox_norm_block(k, s, q_raw, k_raw, qa, ka, cum, half):
    nc = k.nc
    names = ["squares", "mean", "rstd", "act_chain", "dve_chain"]
    squares, mean, rstd_ready, act_chain, dve_chain = map(k.sem, names)
    N = TT * HH
    sq = k.sb(s, "fox_sq", [P, TT * HALF_W])
    ms = k.sb(s, "fox_ms", [P, 2, N])

    def heads(t):
        return t.rearrange("p t (h e) -> p (t h) e", e=HEAD)

    with nc.Block() as block:
        @block.scalar
        def _(act):
            link = Chain(act, act_chain)
            for i, raw in enumerate((q_raw, k_raw)):
                if i:
                    act.wait_ge(mean, i)
                act.activation(sq[:, :], raw[:, :, :].rearrange("p t n -> p (t n)"), ACT.Square).then_inc(squares, 1)
            act.wait_ge(mean, 2)
            link(act.activation(ms[:, :, :], ms[:, :, :], ACT.Ln))
            act.activation(ms[:, :, :], ms[:, :, :], ACT.Exp, scale=-0.5).then_inc(rstd_ready, 1)

        @block.vector
        def _(dve):
            link = Chain(dve, dve_chain)
            for i in range(2):
                dve.wait_ge(squares, i + 1)
                link(dve.tensor_reduce(ms[:, i, :], sq[:, :].rearrange("p (n e) -> p n e", e=HEAD), AX_X, ALU.add))
                dve.tensor_scalar(ms[:, i, :], ms[:, i, :], 1.0 / HEAD, EPS, ALU.mult, ALU.add).then_inc(mean, 1)
            hs = slice(half * HH, (half + 1) * HH)
            dve.memset(qa[:, :, :, HEAD + 1:], 1.0)
            dve.memset(ka[:, :, :, HEAD:HEAD + 1], 1.0)
            dve.tensor_copy(qa[:, :, :, HEAD], cum[:, 0, :, hs])
            dve.tensor_copy(ka[:, :, :, HEAD + 1], cum[:, 1, :, hs])
            dve.wait_ge(rstd_ready, 1)
            for i, (raw, dst) in enumerate(((q_raw, qa), (k_raw, ka))):
                link(dve.tensor_tensor(dst[:, :, :, :].rearrange("p t h e -> p (t h) e")[:, :, :HEAD], heads(raw[:, :, :]),
                                       head_bcast(ms[:, i, :], HEAD), ALU.mult))
    k.clear(names)


def rope(dve, link, cos, sin, src, dst, tmp):
    HR = ROPE // 2
    lead = (slice(None),) * (len(src.shape) - 1)
    z1, z2 = src[lead + (slice(0, HR),)], src[lead + (slice(HR, ROPE),)]
    o1, o2 = dst[lead + (slice(0, HR),)], dst[lead + (slice(HR, ROPE),)]
    a, b, c, e = tmp
    dve.tensor_tensor(a, z1, cos, ALU.mult)
    dve.tensor_tensor(b, z2, sin, ALU.mult)
    dve.tensor_tensor(c, z1, sin, ALU.mult)
    link(dve.tensor_tensor(e, z2, cos, ALU.mult))
    dve.tensor_tensor(o1, a, b, ALU.subtract)
    link(dve.tensor_tensor(o2, c, e, ALU.add))


def mla(k, layer):
    with ExitStack() as outer:
        sg = k.sb(outer, "mla_gate", [P, CT, SEQ])
        mla_inner(k, layer, sg)
        out_block(k, layer, 2, sg, "mla")


def mla_inner(k, layer, sg):
    with ExitStack() as s:
        cqT = k.sb(s, "mla_cqT", [P, Q_RANK // P, SEQ])
        ckvT = k.sb(s, "mla_ckvT", [P, SEQ])
        kr = k.sb(s, "mla_kr", [P, TT, ROPE])
        kr_rot = k.sb(s, "mla_kr_rot", [P, TT, ROPE])
        q_gain = k.sb(s, "mla_q_gain", [MLA_D, 1])
        k_gain = k.sb(s, "mla_k_gain", [MLA_D, 1])
        rope_gain = k.sb(s, "mla_rope_gain", [P, 2, ROPE])
        with ExitStack() as s2:
            lat = k.sb(s2, "mla_lat", [P, TT, Q_RANK + KV_RANK])

            def to_q(eng, ps, t):
                return eng.tensor_copy(lat[:, t, :Q_RANK], ps[:, :Q_RANK])

            def to_kv(eng, ps, t):
                eng.tensor_copy(lat[:, t, Q_RANK:], ps[:, :KV_RANK])
                return eng.tensor_copy(kr[:, t, :], ps[:, KV_RANK:KV_RANK + ROPE])

            project_block(k, layer, [(C_CQ, Q_RANK, "T", ("dve", to_q)),
                                     (C_CKV, KV_RANK + ROPE, "T", ("dve", to_kv))] + gate_jobs(sg, 2, 0, CT), "mla")
            latent_block(k, layer, s2, lat, cqT, ckvT, kr, kr_rot, q_gain, k_gain, rope_gain)
        for half in range(2):
            with ExitStack() as s2:
                v = k.sb(s2, "mla_v", [P, TT, HALF_W])
                q_raw = k.sb(s2, "mla_q", [P, TT, HH, MLA_D])
                k_raw = k.sb(s2, "mla_k", [P, TT, HH, MLA_D])
                expand_block(k, layer, half, cqT, ckvT, kr, kr_rot, rope_gain, v, q_raw, k_raw)
                qT = k.sb(s2, "mla_qT", [MLA_D, HH, SEQ])
                kT = k.sb(s2, "mla_kT", [MLA_D, HH, SEQ])
                turn_block(k, q_raw, k_raw, qT, kT, q_gain, k_gain, MLA_D)
                attention_block(k, qT, kT, v, sg[:, 2 * half:2 * half + 2, :],
                                q_raw[:, :, :, :].rearrange("p t h e -> p (t h e)"),
                                k_raw[:, :, :, :].rearrange("p t h e -> p (t h e)"), "mla")


def latent_block(k, layer, s, lat, cqT, ckvT, kr, kr_rot, q_gain, k_gain, rope_gain):
    nc, d = k.nc, k.dram
    names = ["loaded", "squares", "mean", "rstd", "normed", "turned", "evac", "dve_chain", "act_chain"]
    loaded, squares, mean, rstd_ready, normed, turned, evac, dve_chain, act_chain = map(k.sem, names)
    W = Q_RANK + KV_RANK
    NC = W // P
    gain = k.sb(s, "mla_lat_gain", [P, W])
    sq = k.sb(s, "mla_lat_sq", [P, TT, W])
    ms = k.sb(s, "mla_lat_ms", [P, 2, TT])
    krg = k.sb(s, "mla_krg", [P, TT, ROPE])
    tmp = [k.sb(s, f"mla_kr_tmp{i}", [P, TT, ROPE // 2]) for i in range(4)]
    parts = ((0, Q_RANK), (Q_RANK, W))
    with nc.Block() as block:
        @block.sync
        def _(sp):
            sp.dma_start(gain[:, :Q_RANK], bcast_rows(d["mla_g_cq"][layer], P)).then_inc(loaded, 16)
            sp.dma_start(gain[:, Q_RANK:], bcast_rows(d["mla_g_ckv"][layer], P)).then_inc(loaded, 16)
            for i, (g, name) in enumerate(((q_gain, "mla_g_q"), (k_gain, "mla_g_k"))):
                with nc.allow_non_contiguous_dma(reason="64 gains"):
                    sp.dma_start(g[:HEAD, :], d[name][layer, 0:HEAD].rearrange("(p a) -> p a", a=1)).then_inc(loaded, 16)
                sp.dma_start(rope_gain[:, i, :], bcast_rows(d[name][layer, HEAD:MLA_D], P)).then_inc(loaded, 16)

        @block.scalar
        def _(act):
            link = Chain(act, act_chain)
            act.activation(sq[:, :, :], lat[:, :, :], ACT.Square).then_inc(squares, 1)
            act.wait_ge(mean, 1)
            link(act.activation(ms[:, :, :], ms[:, :, :], ACT.Ln))
            act.activation(ms[:, :, :], ms[:, :, :], ACT.Exp, scale=-0.5).then_inc(rstd_ready, 1)
            for t in range(TT):
                act.wait_ge(turned, t + 1)
                tok = slice(t * P, (t + 1) * P)
                src = k.psum[:, t, :W].rearrange("p (c n) -> p c n", n=P)
                act.activation(cqT[:, :, tok], src[:, :Q_RANK // P, :], ACT.Copy).then_inc(evac, 1)
                act.activation(ckvT[:, tok], src[:, Q_RANK // P, :], ACT.Copy).then_inc(evac, 1)
            act.wait_ge(evac, 2 * TT)

        @block.vector
        def _(dve):
            link = Chain(dve, dve_chain)
            dve.memset(q_gain[HEAD:, :], 1.0)
            link(dve.memset(k_gain[HEAD:, :], 1.0))
            dve.wait_ge(squares, 1)
            for i, (a, b) in enumerate(parts):
                link(dve.tensor_reduce(ms[:, i, :], sq[:, :, a:b], AX_X, ALU.add))
                last = dve.tensor_scalar(ms[:, i, :], ms[:, i, :], 1.0 / (b - a), EPS, ALU.mult, ALU.add)
            last.then_inc(mean, 1)
            dve.wait_ge(loaded, 96)
            dve.wait_ge(rstd_ready, 1)
            for t in range(TT):
                for i, (a, b) in enumerate(parts):
                    last = dve.scalar_tensor_tensor(out=lat[:, t, a:b], in0=lat[:, t, a:b], scalar=ms[:, i, t:t + 1],
                                                    in1=gain[:, a:b], op0=ALU.mult, op1=ALU.mult)
                last.then_inc(normed, 1)
            link(dve.tensor_scalar(q_gain[:, :], q_gain[:, :], MLA_D ** -0.5, None, ALU.mult))
            link(dve.tensor_tensor(krg[:, :, :], kr[:, :, :], rope_gain[:, 1, :].unsqueeze(1).to_broadcast([P, TT, ROPE]),
                                   ALU.mult))
            rope(dve, link, k.cos[:, :, :], k.sin[:, :, :], krg[:, :, :], kr_rot[:, :, :], [x[:, :, :] for x in tmp])

        @block.tensor
        def _(pe):
            for t in range(TT):
                pe.wait_ge(normed, t + 1)
                for c in range(NC):
                    last = pe.transpose(k.psum[:, t, c * P:(c + 1) * P], lat[:, t, c * P:(c + 1) * P], k.ident[:, :])
                last.then_inc(turned, 1)
    k.clear(names)


def expand_block(k, layer, half, cqT, ckvT, kr, kr_rot, rope_gain, v, q_raw, k_raw):
    nc, d = k.nc, k.dram
    names = ["loaded", "q_product", "kv_product", "q_evac", "kv_evac", "squares", "mean", "rstd", "dve_chain", "act_chain"]
    loaded, q_product, kv_product, q_evac, kv_evac, squares, mean, rstd_ready, dve_chain, act_chain = map(k.sem, names)
    QW, KVW, N, HR = HH * MLA_D, HH * 2 * HEAD, TT * HH, ROPE // 2
    NQ = Q_RANK // P
    with ExitStack() as s:
        w_uq = k.sb(s, "mla_w_uq", [P, NQ, QW])
        w_ukv = k.sb(s, "mla_w_ukv", [P, KVW])
        sq = k.sb(s, "mla_sq", [P, N, MLA_D])
        ms = k.sb(s, "mla_ms", [P, 2, N])
        rot = k.sb(s, "mla_rot", [P, TT, HH, ROPE])
        tmp = [sq[:, :, :].rearrange("p n e -> p (n e)")[:, i * N * HR:(i + 1) * N * HR]
               .rearrange("p (t h e) -> p t h e", t=TT, h=HH) for i in range(4)]
        with nc.Block() as block:
            @block.sync
            def _(sp):
                sp.dma_start(w_uq[:, :, :], d["mla_w_uq"][layer].rearrange("(c p) n -> p c n", p=P)
                             [:, :, half * QW:(half + 1) * QW]).then_inc(loaded, 16)
                sp.dma_start(w_ukv[:, :], d["mla_w_ukv"][layer][:, half * KVW:(half + 1) * KVW]).then_inc(loaded, 16)

            @block.tensor
            def _(pe):
                pe.wait_ge(loaded, 32)
                for t in range(TT):
                    tok = slice(t * P, (t + 1) * P)
                    if t >= 4:
                        pe.wait_ge(q_evac, t - 3)
                        pe.wait_ge(kv_evac, t - 3)
                    for c in range(NQ):
                        last = pe.matmul(k.psum[:, t % 4, :QW], cqT[:, c, tok], w_uq[:, c, :], start=(c == 0),
                                         stop=(c == NQ - 1))
                    last.then_inc(q_product, 1)
                    pe.matmul(k.psum[:, 4 + t % 4, :KVW], ckvT[:, tok], w_ukv[:, :], start=True, stop=True)\
                      .then_inc(kv_product, 1)

            @block.scalar
            def _(act):
                link = Chain(act, act_chain)
                for t in range(TT):
                    act.wait_ge(q_product, t + 1)
                    act.activation(q_raw[:, t, :, :].rearrange("p h e -> p (h e)"), k.psum[:, t % 4, :QW], ACT.Copy)\
                       .then_inc(q_evac, 1)
                act.wait_ge(q_evac, TT)
                act.activation(sq[:, :, :], q_raw[:, :, :, :].rearrange("p t h e -> p (t h) e"), ACT.Square)\
                   .then_inc(squares, 1)
                act.wait_ge(kv_evac, TT + 1)
                act.wait_ge(mean, 1)
                act.activation(sq[:, :, :], k_raw[:, :, :, :].rearrange("p t h e -> p (t h) e"), ACT.Square)\
                   .then_inc(squares, 1)
                act.wait_ge(mean, 2)
                link(act.activation(ms[:, :, :], ms[:, :, :], ACT.Ln))
                act.activation(ms[:, :, :], ms[:, :, :], ACT.Exp, scale=-0.5).then_inc(rstd_ready, 1)

            @block.vector
            def _(dve):
                link = Chain(dve, dve_chain)
                for t in range(TT):
                    dve.wait_ge(kv_product, t + 1)
                    src = k.psum[:, 4 + t % 4, :].rearrange("p (h e) -> p h e", h=HH)
                    dve.tensor_copy(k_raw[:, t, :, :HEAD], src[:, :, :HEAD])
                    dve.tensor_copy(v[:, t, :].rearrange("p (h e) -> p h e", h=HH), src[:, :, HEAD:]).then_inc(kv_evac, 1)
                dve.tensor_copy(k_raw[:, :, :, HEAD:], kr[:, :, :].unsqueeze(2).to_broadcast([P, TT, HH, ROPE]))\
                   .then_inc(kv_evac, 1)
                for i in range(2):
                    dve.wait_ge(squares, i + 1)
                    link(dve.tensor_reduce(ms[:, i, :], sq[:, :, :], AX_X, ALU.add))
                    dve.tensor_scalar(ms[:, i, :], ms[:, i, :], 1.0 / MLA_D, EPS, ALU.mult, ALU.add).then_inc(mean, 1)
                dve.wait_ge(rstd_ready, 1)
                q_all = q_raw[:, :, :, :].rearrange("p t h e -> p (t h) e")
                k_all = k_raw[:, :, :, :].rearrange("p t h e -> p (t h) e")
                link(dve.tensor_tensor(q_all, q_all, head_bcast(ms[:, 0, :], MLA_D), ALU.mult))
                link(dve.tensor_tensor(k_all[:, :, :HEAD], k_all[:, :, :HEAD], head_bcast(ms[:, 1, :], HEAD), ALU.mult))
                dve.tensor_tensor(k_raw[:, :, :, HEAD:], kr_rot[:, :, :].unsqueeze(2).to_broadcast([P, TT, HH, ROPE]),
                                  ms[:, 1, :].rearrange("p (t h) -> p t h", h=HH).unsqueeze(3)
                                  .to_broadcast([P, TT, HH, ROPE]), ALU.mult)
                link(dve.tensor_tensor(rot[:, :, :, :].rearrange("p t h e -> p (t h) e"), q_all[:, :, HEAD:],
                                       rope_gain[:, 0, :].unsqueeze(1).to_broadcast([P, N, ROPE]), ALU.mult))

                def over_heads(x):
                    return x[:, :, :].unsqueeze(2).to_broadcast([P, TT, HH, HR])

                rope(dve, link, over_heads(k.cos), over_heads(k.sin), rot[:, :, :, :], q_raw[:, :, :, HEAD:], tmp)
    k.clear(names)


def lru(k, layer):
    with ExitStack() as s:
        sg = k.sb(s, "lru_gate", [P, CT, SEQ])
        with ExitStack() as s2:
            PAD = CONV_W - 1
            dx = k.sb(s2, "lru_dx", [P, CT, PAD + SEQ])

            def to_dx(i):
                def evac(eng, ps, mn):
                    m, n = mn
                    return eng.tensor_copy(dx[:, 2 * i + m, PAD + n * BANK:PAD + (n + 1) * BANK], ps)
                return ("dve", evac)

            project_block(k, layer, [(C_DX + i * CHUNK, CHUNK, "C", to_dx(i)) for i in range(GROUP_W // CHUNK)]
                          + gate_jobs(sg, 3, 0, CT), "lru")
            lru_block(k, layer, s2, dx, sg)
        out_block(k, layer, 3, sg, "lru")


def lru_block(k, layer, s, dx, sg):
    nc, d = k.nc, k.dram
    names = ["loaded", "zeroed", "blocks_landed", "conv_done", "r_product", "i_product", "r_ready", "i_ready", "rate",
             "tau_ready", "a_ready", "square", "u_ready", "root", "used", "scanned", "dve_chain", "act_chain", "handover"]
    (loaded, zeroed, blocks_landed, conv_done, r_product, i_product, r_ready, i_ready, rate, tau_ready, a_ready, square,
     u_ready, root, used, scanned, dve_chain, act_chain, handover) = map(k.sem, names)
    PAD, NH = CONV_W - 1, SEQ // BANK
    xc = k.sb(s, "lru_xc", [P, CT, SEQ])
    r = k.sb(s, "lru_r", [P, CT, SEQ])
    i_g = k.sb(s, "lru_i", [P, CT, SEQ])
    a2 = k.sb(s, "lru_a2", [P, 2, SEQ])
    w_bd = [k.sb(s, f"lru_w_{n}", [P, CT, P]) for n in "ri"]
    conv_w = k.sb(s, "lru_conv_w", [P, CONV_W, CT])
    vec = k.sb(s, "lru_vec", [P, 4, CT])
    small = k.sb(s, "lru_small", [P, 4, CT])
    tau = dx
    with nc.Block() as block:
        @block.sync
        def _(sp):
            with nc.allow_non_contiguous_dma(reason="per-channel vectors"):
                for j in range(CONV_W):
                    sp.dma_start(conv_w[:, j, :], d["lru_conv_w"][layer, j, :].rearrange("(m p) -> p m", p=P))\
                      .then_inc(loaded, 16)
                for j, name in enumerate(("lru_conv_b", "lru_b_r", "lru_b_i", "lru_lam")):
                    sp.dma_start(vec[:, j, :], d[name][layer].rearrange("(m p) -> p m", p=P)).then_inc(loaded, 16)
            sp.wait_ge(zeroed, 1)
            for w, name in zip(w_bd, ("lru_w_r", "lru_w_i")):
                src = d[name][layer].rearrange("(m b) c e -> b c m e", b=2)
                for b in range(2):
                    sp.dma_start(w[b * HEAD:(b + 1) * HEAD, :, b * HEAD:(b + 1) * HEAD], src[b]).then_inc(blocks_landed, 16)

        @block.gpsimd
        def _(pool):
            pool.memset(w_bd[0][:, :, :], 0.0)
            pool.memset(w_bd[1][:, :, :], 0.0).then_inc(zeroed, 1)

        @block.tensor
        def _(pe):
            pe.wait_ge(blocks_landed, 64)
            for m in range(CT):
                pe.wait_ge(conv_done, m + 1)
                for n in range(NH):
                    u = m * NH + n
                    for g, (w, done, taken) in enumerate(((w_bd[0], r_product, r_ready), (w_bd[1], i_product, i_ready))):
                        if u >= 4:
                            pe.wait_ge(taken, u - 3)
                        pe.matmul(k.psum[:, 4 * g + u % 4, :], w[:, m, :], xc[:, m, n * BANK:(n + 1) * BANK],
                                  start=True, stop=True).then_inc(done, 1)

        @block.vector
        def _(dve):
            link = Chain(dve, dve_chain)
            link(dve.memset(dx[:, :, :PAD], 0.0))
            dve.wait_ge(loaded, 128)
            link(dve.tensor_scalar(small[:, 0, :], vec[:, 3, :], -1.0, None, ALU.mult))
            dve.tensor_tensor(small[:, 1, :], small[:, 0, :], vec[:, 3, :], ALU.max).then_inc(handover, 1)
            for m in range(CT):
                link(dve.tensor_scalar(xc[:, m, :], dx[:, m, 0:SEQ], conv_w[:, 0, m:m + 1], vec[:, 0, m:m + 1],
                                       ALU.mult, ALU.add))
                for j in range(1, CONV_W):
                    link(dve.scalar_tensor_tensor(out=xc[:, m, :], in0=dx[:, m, j:j + SEQ], scalar=conv_w[:, j, m:m + 1],
                                                  in1=xc[:, m, :], op0=ALU.mult, op1=ALU.add))
                dve.sem_inc(conv_done, 1)
                if m == 0:
                    dve.wait_ge(handover, 2)
                    link(dve.scalar_tensor_tensor(out=small[:, 2, :], in0=small[:, 0, :], scalar=0.0,
                                                  in1=small[:, 1, :], op0=ALU.max, op1=ALU.add))
                    link(dve.tensor_scalar(small[:, 2, :], small[:, 2, :], LRU_C, None, ALU.mult))
                    dve.tensor_scalar(small[:, 3, :], small[:, 2, :], -1.0, None, ALU.mult).then_inc(rate, 1)
            for m in range(CT):
                dve.wait_ge(i_ready, NH * (m + 1))
                dve.wait_ge(r_product, NH * (m + 1))
                dve.wait_ge(i_product, NH * (m + 1))
                link(dve.tensor_tensor(xc[:, m, :], xc[:, m, :], i_g[:, m, :], ALU.mult))
            for m in range(CT):
                dve.wait_ge(square, m + 1)
                dve.wait_ge(tau_ready, m + 1)
                dve.scalar_tensor_tensor(out=tau[:, m, :SEQ], in0=a2[:, m % 2, :], scalar=1.0, in1=tau[:, m, :SEQ],
                                         op0=ALU.add, op1=ALU.mult).then_inc(u_ready, 1)
            for m in range(CT):
                dve.wait_ge(root, m + 1)
                link(dve.tensor_tensor(xc[:, m, :], xc[:, m, :], tau[:, m, :SEQ], ALU.mult))
                link(dve.tensor_tensor_scan(i_g[:, m, :], r[:, m, :], xc[:, m, :], 0.0, ALU.mult, ALU.add))
                link(dve.tensor_tensor(sg[:, m, :], sg[:, m, :], i_g[:, m, :], ALU.mult))

        @block.scalar
        def _(act):
            link = Chain(act, act_chain)
            act.wait_ge(handover, 1)
            link(act.activation(small[:, 1, :], small[:, 1, :], ACT.Exp, scale=-1.0))
            act.activation(small[:, 1, :], small[:, 1, :], ACT.Ln, bias=1.0).then_inc(handover, 1)
            for m in range(CT):
                for n in range(NH):
                    u = m * NH + n
                    at = slice(n * BANK, (n + 1) * BANK)
                    act.wait_ge(r_product, u + 1)
                    act.activation(r[:, m, at], k.psum[:, u % 4, :], ACT.Sigmoid, bias=vec[:, 1, m:m + 1]).then_inc(r_ready, 1)
                    act.wait_ge(i_product, u + 1)
                    act.activation(i_g[:, m, at], k.psum[:, 4 + u % 4, :], ACT.Sigmoid, bias=vec[:, 2, m:m + 1])\
                       .then_inc(i_ready, 1)
            act.wait_ge(rate, 1)
            act.wait_ge(conv_done, CT)
            act.wait_ge(r_ready, NH * CT)
            for m in range(CT):
                act.activation(tau[:, m, :SEQ], r[:, m, :], ACT.Tanh, scale=small[:, 2, m:m + 1]).then_inc(tau_ready, 1)
                link(act.activation(r[:, m, :], r[:, m, :], ACT.Exp, scale=small[:, 3, m:m + 1]))
                if m >= 2:
                    act.wait_ge(u_ready, m - 1)
                act.activation(a2[:, m % 2, :], r[:, m, :], ACT.Square).then_inc(square, 1)
            for m in range(CT):
                act.wait_ge(u_ready, m + 1)
                act.activation(tau[:, m, :SEQ], tau[:, m, :SEQ], ACT.Sqrt).then_inc(root, 1)
    k.clear(names)


def store_block(k):
    with k.nc.Block() as block:
        @block.sync
        def _(sp):
            stored = k.sem("stored")
            sp.dma_start(k.out[0].rearrange("(t p) n -> p t n", p=P), k.x[:, :, :]).then_inc(stored, 16)
            sp.wait_ge(stored, 16)


def trunk_kernel(nc, dram, out, parts="ABCD"):
    with ExitStack() as ctx:
        k = Trunk(nc, dram, out, ctx)
        setup_block(k)
        with nc.Fori(0, DEPTH) as layer:
            norm_block(k, layer)
            if "A" in parts:
                gla(k, layer)
            if "B" in parts:
                fox(k, layer)
            if "C" in parts:
                mla(k, layer)
            if "D" in parts:
                lru(k, layer)
        store_block(k)


def constants():
    i = np.arange(P)
    masks = np.zeros((P, LEVELS, P), np.int32)
    for j in range(LEVELS):
        B = 64 >> j
        half = (i // B) % 2
        masks[:, j, :] = (i[:, None] // (2 * B) == i[None, :] // (2 * B)) & (half[:, None] == 0) & (half[None, :] == 1)
    bf16 = mybir.dt.np(BF16)
    freq = (10000.0 ** (-np.arange(ROPE // 2, dtype=np.float32) / np.float32(ROPE // 2))).astype(np.float32)
    return {
        "c_ident": np.eye(P, dtype=np.float32),
        "c_ident_bf": np.eye(P, dtype=np.float32).astype(bf16),
        "c_mask_bf": np.where(i[:, None] >= i[None, :], 0.0, NEG).astype(np.float32).astype(bf16),
        "c_upper": (i[:, None] <= i[None, :]).astype(np.float32),
        "c_masks": masks,
        "c_head_mask": (i[:, None] // DK == np.arange(HH)[None, :]).astype(np.float32),
        "c_freq": np.tile(freq[None, :], (P, 1)),
    }


_INS = ["x", "positions", "norm_g", "w_in", "w_out", "gla_w_up", "gla_b_up", "gla_g_out", "fox_b_f", "fox_g_q",
        "fox_g_k", "mla_g_cq", "mla_w_uq", "mla_g_ckv", "mla_w_ukv", "mla_g_q", "mla_g_k", "lru_conv_w",
        "lru_conv_b", "lru_w_r", "lru_b_r", "lru_w_i", "lru_b_i", "lru_lam"]


def kernel(**inputs):
    import concourse.bacc as bacc
    from concourse.bass_utils import run_bass_kernel_spmd

    nc = bacc.Bacc("TRN2", target_bir_lowering=False, num_devices=1)
    arrays, dram = {}, {}
    for name, a in list((n, inputs[n]) for n in _INS) + list(constants().items()):
        a = np.ascontiguousarray(a)
        arrays[f"in_{name}_dram"] = a
        dram[name] = nc.dram_tensor(f"in_{name}_dram", a.shape, mybir.dt.from_np(a.dtype), kind="ExternalInput").ap()
    out = nc.dram_tensor("out_0_dram", (1, SEQ, D_MODEL), F32, kind="ExternalOutput").ap()
    trunk_kernel(nc, dram, out)
    r = run_bass_kernel_spmd(nc, [arrays], core_ids=[0])
    return r.results[0]["out_0_dram"]
```

```python
from contextlib import ExitStack

import numpy as np

import concourse.bass as bass
from concourse import mybir

ALU = mybir.AluOpType
ACT = mybir.ActivationFunctionType
F32 = mybir.dt.float32
F32R = mybir.dt.float32r
BF16 = mybir.dt.bfloat16
I32 = mybir.dt.int32
AX_X = mybir.AxisListType.X

P = 128
BANK = 512
D_MODEL, SEQ, DEPTH = 1024, 1024, 2
KT = D_MODEL // P
TT = SEQ // P
D_MIX = 2 * D_MODEL
GROUP_W = D_MIX // 4
HEAD = 64
HEADS = GROUP_W // HEAD
HH = 4
HALF_W = HH * HEAD
CT = GROUP_W // P
EPS = 1e-6
DK, RANK = HEAD // 2, 16
GN = HEADS * DK // P
LEVELS = 7
Q_RANK, KV_RANK, ROPE = D_MODEL // 4, D_MODEL // 8, HEAD // 2
MLA_D = HEAD + ROPE
FOX_D = HEAD + 2
CONV_W, LRU_C = 4, 8.0
NEG = -1e30

IN_SIZES = (D_MIX, 256, 256, 512, RANK, 512, 512, 512, HEADS, Q_RANK, KV_RANK, ROPE, GROUP_W)
COL = np.concatenate([[0], np.cumsum(IN_SIZES)]).tolist()
(C_GATE, C_AQ, C_AK, C_AV, C_AG, C_BQ, C_BK, C_BV, C_BF, C_CQ, C_CKV, C_CKR, C_DX, D_IN) = COL
CHUNK = 256
CHUNK_MAX = CHUNK + RANK
WARM_PRODUCTS = 16


class Trunk:

    def __init__(self, nc, dram, out, ctx):
        self.nc, self.dram, self.out, self.ctx = nc, dram, out, ctx
        self.sems, self.used = {}, {}
        self.x = self.sb(ctx, "x_res", [P, TT, D_MODEL])
        self.h_hi = self.sb(ctx, "h_hi", [P, KT, SEQ], F32R)
        self.h_lo = self.sb(ctx, "h_lo", [P, KT, SEQ], F32R)
        self.ident = self.sb(ctx, "ident", [P, P])
        self.ident_bf = self.sb(ctx, "ident_bf", [P, P], BF16)
        self.mask_bf = self.sb(ctx, "mask_bf", [P, P], BF16)
        self.cos = self.sb(ctx, "cos", [P, TT, ROPE // 2])
        self.sin = self.sb(ctx, "sin", [P, TT, ROPE // 2])
        self.w_next = self.sb(ctx, "w_next", [P, KT * CHUNK_MAX])
        self.w_next_landed = ctx.enter_context(nc.semaphore("w_next_landed"))
        self.plan, self.at = weight_plan(), 0
        self.psum = ctx.enter_context(nc.psum_tensor("psum", [P, 8, BANK], F32))

    def sb(self, ctx, name, shape, dt=F32):
        self.used[name] = self.used.get(name, 0) + 1
        name += f"_{self.used[name]}" if self.used[name] > 1 else ""
        return ctx.enter_context(self.nc.sbuf_tensor(name, shape, dt))

    def sem(self, name):
        if name not in self.sems:
            self.sems[name] = self.ctx.enter_context(self.nc.semaphore(name))
        return self.sems[name]

    def fetch(self, eng, layer, item):
        kind, a, width = item
        if kind == "w_in":
            src = self.dram["w_in"][layer].rearrange("(k p) n -> p k n", p=P)[:, :, a:a + width]
        else:
            src = w_out_rows(self, layer, a)[:, :, :BANK]
        eng.dma_start(self.next_view(item), src).then_inc(self.w_next_landed, 16)

    def next_view(self, item):
        n, width = (KT, item[2]) if item[0] == "w_in" else (CT, BANK)
        return self.w_next[:, :n * width].rearrange("p (k n) -> p k n", n=width)

    def take(self, item):
        assert self.plan[self.at] == item, (self.plan[self.at], item)
        self.at += 1
        return self.next_view(item)

    def clear(self, names, fetch_for=None):
        with self.nc.Block() as block:
            @block.gpsimd
            def _(pool):
                for n in names:
                    pool.sem_clear(self.sems[n])

            @block.sync
            def _(sp):
                if fetch_for is not None:
                    sp.sem_clear(self.w_next_landed)
                    if self.at < len(self.plan):
                        self.fetch(sp, fetch_for, self.plan[self.at])


def weight_plan():
    gates = [("w_in", C_GATE + i * CHUNK, CHUNK) for i in range(D_MIX // CHUNK)]
    return [
        ("w_in", C_AQ, CHUNK), gates[0], gates[1], ("w_out", 0, BANK),
        ("w_in", C_BQ + HALF_W, HALF_W), gates[3], ("w_in", C_BQ, HALF_W), gates[2], ("w_out", 1, BANK),
        ("w_in", C_CQ, Q_RANK), gates[4], gates[5], ("w_out", 2, BANK),
        ("w_in", C_DX, CHUNK), gates[6], gates[7], ("w_out", 3, BANK),
    ]


class Chain:

    def __init__(self, eng, sem):
        self.eng, self.sem, self.n = eng, sem, 0

    def __call__(self, ins):
        self.n += 1
        ins.then_inc(self.sem, 1)
        self.eng.wait_ge(self.sem, self.n)
        return ins


def warm_clock(k, pe, bank):
    for _ in range(WARM_PRODUCTS):
        pe.matmul(k.psum[:, bank, :], k.h_hi[:, 0, :P], k.h_hi[:, 0, :BANK], start=True, stop=True)


def bcast_rows(ap, n):
    return ap.rearrange("(a m) -> a m", a=1).to_broadcast([n, ap.shape[0]])


def head_bcast(ap, n):
    return ap.unsqueeze(2).to_broadcast([ap.shape[0], ap.shape[1], n])


def setup_block(k):
    nc, d = k.nc, k.dram
    HR = ROPE // 2
    loaded, step, stepped, act_step = (k.sem(n) for n in ("loaded", "dve_chain", "handover", "act_chain"))
    TWO_PI = 2.0 * np.pi
    C1 = float(np.float32(6.28125))
    C2 = 8116.0 / 2 ** 22
    C3 = float(np.float32(TWO_PI - C1 - C2))
    MAGIC = float(1.5 * 2 ** 23)
    with ExitStack() as s:
        pos_i = k.sb(s, "pos_i", [P, TT], I32)
        pos_f = k.sb(s, "pos_f", [P, TT])
        freq = k.sb(s, "freq", [P, HR])
        ang = k.sb(s, "ang", [P, TT, HR])
        turns = k.sb(s, "turns", [P, TT, HR])
        comp = k.sb(s, "comp", [P, TT, HR])
        low = k.sb(s, "low", [P, TT, HR])
        with nc.Block() as block:
            @block.sync
            def _(sp):
                sp.dma_start(k.x[:, :, :], d["x"][0].rearrange("(t p) n -> p t n", p=P)).then_inc(loaded, 16)
                sp.dma_start(k.ident[:, :], d["c_ident"]).then_inc(loaded, 16)
                sp.dma_start(k.ident_bf[:, :], d["c_ident_bf"]).then_inc(loaded, 16)
                sp.dma_start(k.mask_bf[:, :], d["c_mask_bf"]).then_inc(loaded, 16)
                sp.dma_start(freq[:, :], d["c_freq"]).then_inc(loaded, 16)
                with nc.allow_non_contiguous_dma(reason="4 KB of positions"):
                    sp.dma_start(pos_i[:, :], d["positions"][0].rearrange("(t p) -> p t", p=P)).then_inc(loaded, 16)
                sp.wait_ge(loaded, 96)

            @block.vector
            def _(dve):
                link = Chain(dve, step)
                dve.wait_ge(loaded, 96)
                link(dve.tensor_copy(pos_f[:, :], pos_i[:, :]))
                link(dve.tensor_tensor(ang[:, :, :], head_bcast(pos_f[:, :], HR),
                                       freq[:, :].unsqueeze(1).to_broadcast([P, TT, HR]), ALU.mult))
                link(dve.tensor_scalar(turns[:, :, :], ang[:, :, :], 1.0 / TWO_PI, MAGIC, ALU.mult, ALU.add))
                link(dve.tensor_scalar(turns[:, :, :], turns[:, :, :], -MAGIC, None, ALU.add))
                for c in (C1, C2, C3):
                    link(dve.scalar_tensor_tensor(out=ang[:, :, :], in0=turns[:, :, :], scalar=-c, in1=ang[:, :, :],
                                                  op0=ALU.mult, op1=ALU.add))
                link(dve.tensor_scalar(turns[:, :, :], ang[:, :, :], -1.0, None, ALU.mult))
                link(dve.tensor_tensor(comp[:, :, :], turns[:, :, :], ang[:, :, :], ALU.max))
                dve.tensor_scalar(turns[:, :, :], ang[:, :, :], -1.0, float(np.pi), ALU.mult, ALU.add)
                link(dve.tensor_scalar(low[:, :, :], ang[:, :, :], -1.0, -float(np.pi), ALU.mult, ALU.add))
                link(dve.tensor_tensor(ang[:, :, :], ang[:, :, :], turns[:, :, :], ALU.min))
                link(dve.tensor_tensor(ang[:, :, :], ang[:, :, :], low[:, :, :], ALU.max))
                dve.tensor_scalar(comp[:, :, :], comp[:, :, :], -1.0, float(np.pi / 2), ALU.mult, ALU.add)\
                   .then_inc(stepped, 1)

            @block.scalar
            def _(act):
                act.wait_ge(stepped, 1)
                act.activation(k.sin[:, :, :], ang[:, :, :], ACT.Sin)
                act.activation(k.cos[:, :, :], comp[:, :, :], ACT.Sin).then_inc(act_step, 1)
                act.wait_ge(act_step, 1)
    k.clear(["loaded", "dve_chain", "handover", "act_chain"])


def norm_block(k, layer):
    nc, d = k.nc, k.dram
    names = ["loaded", "squares", "mean", "rstd", "act_chain", "normed", "transposed", "hi_done", "lo_done", "dve_chain"]
    loaded, squares, mean, rstd_ready, act_chain, normed, transposed, hi_done, lo_done, dve_chain = map(k.sem, names)
    with ExitStack() as s:
        gain = k.sb(s, "norm_gain", [P, D_MODEL])
        sq = k.sb(s, "norm_sq", [P, D_MODEL])
        ss = k.sb(s, "norm_ss", [P, TT])
        ms = k.sb(s, "norm_ms", [P, TT])
        rstd = k.sb(s, "norm_rstd", [P, TT])
        xn = k.sb(s, "norm_xn", [P, 2, D_MODEL])
        with nc.Block() as block:
            @block.sync
            def _(sp):
                sp.dma_start(gain[:, :], bcast_rows(d["norm_g"][layer], P)).then_inc(loaded, 16)
                k.fetch(sp, layer, k.plan[0])

            @block.scalar
            def _(act):
                link = Chain(act, act_chain)
                for t in range(TT):
                    link(act.activation(sq[:, :], k.x[:, t, :], ACT.Square, accum_out=ss[:, t:t + 1]))
                act.sem_inc(squares, 1)
                act.wait_ge(mean, 1)
                link(act.activation(rstd[:, :], ms[:, :], ACT.Ln))
                act.activation(rstd[:, :], rstd[:, :], ACT.Exp, scale=-0.5).then_inc(rstd_ready, 1)
                for t in range(TT):
                    for j in range(2):
                        u = 2 * t + j
                        act.wait_ge(transposed, u + 1)
                        src = k.psum[:, u % 8, :].rearrange("p (c n) -> p c n", c=4)
                        act.activation(k.h_hi[:, 4 * j:4 * j + 4, t * P:(t + 1) * P], src, ACT.Copy)\
                           .then_inc(hi_done, 1)

            @block.vector
            def _(dve):
                link = Chain(dve, dve_chain)
                dve.wait_ge(squares, 1)
                dve.tensor_scalar(ms[:, :], ss[:, :], 1.0 / D_MODEL, EPS, ALU.mult, ALU.add).then_inc(mean, 1)
                dve.wait_ge(rstd_ready, 1)
                dve.wait_ge(loaded, 16)
                for t in range(TT + 1):
                    if t < TT:
                        if t >= 2:
                            dve.wait_ge(transposed, 2 * (t - 1))
                        dve.scalar_tensor_tensor(out=xn[:, t % 2, :], in0=k.x[:, t, :], scalar=rstd[:, t:t + 1],
                                                 in1=gain[:, :], op0=ALU.mult, op1=ALU.mult).then_inc(normed, 1)
                    if t >= 1:
                        for j in range(2):
                            u = 2 * (t - 1) + j
                            dve.wait_ge(hi_done, u + 1)
                            at = (slice(None), slice(4 * j, 4 * j + 4), slice((t - 1) * P, t * P))
                            src = k.psum[:, u % 8, :].rearrange("p (c n) -> p c n", c=4)
                            dve.tensor_tensor(k.h_lo[at], src, k.h_hi[at].bitcast(F32), ALU.subtract)\
                               .then_inc(lo_done, 1)

            @block.tensor
            def _(pe):
                for t in range(TT):
                    pe.wait_ge(normed, t + 1)
                    for j in range(2):
                        u = 2 * t + j
                        if u >= 8:
                            pe.wait_ge(lo_done, u - 7)
                        for c in range(4):
                            kk = 4 * j + c
                            last = pe.transpose(k.psum[:, u % 8, c * P:(c + 1) * P],
                                                xn[:, t % 2, kk * P:(kk + 1) * P], k.ident[:, :])
                        last.then_inc(transposed, 1)
    k.clear(names)


def project_block(k, layer, jobs, tag, side=None):
    nc, d = k.nc, k.dram
    names = ["w_landed0", "w_landed1", "w_hi", "w_lo", "unit_done", "act_evac", "dve_evac"]
    w_landed0, w_landed1, w_hi_ready, w_lo_ready, unit_done, act_evac, dve_evac = map(k.sem, names)
    w_landed = [w_landed0, w_landed1]
    w_in = d["w_in"][layer].rearrange("(k p) n -> p k n", p=P)
    units = []
    for j, (col, width, kind, evac) in enumerate(jobs):
        parts = [(m, n) for m in range(width // P) for n in range(SEQ // BANK)] if kind == "C" else range(TT)
        units += [(j, part) for part in parts]
    by = [jobs[j][3][0] for j, _ in units]
    nth = [by[:u + 1].count(by[u]) for u in range(len(units))]
    evac_sem = {"act": act_evac, "dve": dve_evac}
    first_unit = [next(i for i, (jj, _) in enumerate(units) if jj == j) for j in range(len(jobs))] + [len(units)]
    ring = min(2, len(jobs))
    assert side is None or (len(jobs) <= 2 and len(units) <= 8 and set(by) == {"act"})
    with ExitStack() as s:
        wide = max(job[1] for job in jobs)
        if len(jobs) > 1:
            raw = k.sb(s, tag + "_w_raw", [P, ring, KT, wide])
        hi = k.sb(s, tag + "_w_hi", [P, ring, KT, wide], F32R)
        lo = k.sb(s, tag + "_w_lo", [P, ring, KT, wide], F32R)
        chunk0 = k.take(("w_in", jobs[0][0], jobs[0][1]))

        def chunk(j):
            return chunk0 if j == 0 else raw[:, j % ring, :, :jobs[j][1]]

        with nc.Block() as block:
            @block.sync
            def _(sp):
                for j, (col, width, kind, evac) in enumerate(jobs[1:], 1):
                    if j >= 3:
                        sp.wait_ge(w_lo_ready, j - 1)
                    sp.dma_start(chunk(j), w_in[:, :, col:col + width]).then_inc(w_landed[j % 2], 16)

            def evacuate(eng, me, first, end):
                for u in range(first, end):
                    if by[u] == me:
                        j, part = units[u]
                        eng.wait_ge(unit_done, u + 1)
                        jobs[j][3][1](eng, k.psum[:, u % 8, :], part).then_inc(evac_sem[me], 1)

            @block.scalar
            def _(act):
                def round_chunk(j):
                    width = jobs[j][1]
                    if j == 0:
                        act.wait_ge(k.w_next_landed, 16)
                    else:
                        act.wait_ge(w_landed[j % 2], 16 * ((j + 1) // 2))
                    if j >= 2:
                        act.wait_ge(unit_done, first_unit[j - 1])
                    act.activation(hi[:, j % ring, :, :width], chunk(j), ACT.Copy).then_inc(w_hi_ready, 1)

                if side is not None:
                    for j in range(len(jobs)):
                        round_chunk(j)
                    side.scalar(act)
                    evacuate(act, "act", 0, len(units))
                    return
                for j in range(len(jobs) + 1):
                    if j < len(jobs):
                        round_chunk(j)
                    if j >= 1:
                        evacuate(act, "act", first_unit[j - 1], first_unit[j])

            @block.gpsimd
            def _(pool):
                for j, (col, width, kind, evac) in enumerate(jobs):
                    pool.wait_ge(w_hi_ready, j + 1)
                    pool.tensor_tensor(lo[:, j % ring, :, :width], chunk(j), hi[:, j % ring, :, :width].bitcast(F32),
                                       ALU.subtract).then_inc(w_lo_ready, 1)
                pool.wait_ge(w_lo_ready, len(jobs))

            @block.vector
            def _(dve):
                if side is not None:
                    side.vector(dve, act_evac)
                else:
                    evacuate(dve, "dve", 0, len(units))

            @block.tensor
            def _(pe):
                for u, (j, part) in enumerate(units):
                    width, kind = jobs[j][1], jobs[j][2]
                    if u == first_unit[j]:
                        pe.wait_ge(w_hi_ready, j + 1)
                    if u >= 8:
                        pe.wait_ge(evac_sem[by[u - 8]], nth[u - 8])
                    for n, (w, h) in enumerate(((hi, k.h_hi), (hi, k.h_lo), (lo, k.h_hi))):
                        if n == 2 and u == first_unit[j]:
                            pe.wait_ge(w_lo_ready, j + 1)
                        for kk in range(KT):
                            if kind == "C":
                                m, half = part
                                lhsT = w[:, j % ring, kk, m * P:(m + 1) * P]
                                rhs, o = h[:, kk, half * BANK:(half + 1) * BANK], k.psum[:, u % 8, :]
                            else:
                                lhsT, rhs = h[:, kk, part * P:(part + 1) * P], w[:, j % ring, kk, :width]
                                o = k.psum[:, u % 8, :width]
                            last = pe.matmul(o, lhsT, rhs, start=(kk == 0 and n == 0), stop=(kk == KT - 1 and n == 2))
                    last.then_inc(unit_done, 1)
    k.clear(names + (side.names if side is not None else []), fetch_for=layer)


class Side:

    def __init__(self, names, scalar, vector):
        self.names, self.scalar, self.vector = names, scalar, vector


def w_out_rows(k, layer, mixer):
    r0 = mixer * GROUP_W
    return k.dram["w_out"][layer, r0:r0 + GROUP_W, :].rearrange("(c p) n -> p c n", p=P)


def out_block(k, layer, mixer, y, tag):
    nc = k.nc
    names = ["w_landed", "w_hi", "w_lo", "y_hi", "y_lo", "unit_done", "added"]
    w_landed, w_hi_ready, w_lo_ready, y_hi_ready, y_lo_ready, unit_done, added = map(k.sem, names)
    NQ = D_MODEL // BANK
    units = [(n, t) for n in range(NQ) for t in range(TT)]
    with ExitStack() as s:
        w_second = k.sb(s, tag + "_wo_raw", [P, CT, BANK])
        w_raw = [k.take(("w_out", mixer, BANK)), w_second[:, :, :]]
        w_hi = k.sb(s, tag + "_wo_hi", [P, CT, D_MODEL], F32R)
        w_lo = k.sb(s, tag + "_wo_lo", [P, CT, D_MODEL], F32R)
        y_hi = k.sb(s, tag + "_y_hi", [P, CT, SEQ], F32R)
        y_lo = k.sb(s, tag + "_y_lo", [P, CT, SEQ], F32R)

        def half(n):
            return slice(n * BANK, (n + 1) * BANK)

        with nc.Block() as block:
            @block.sync
            def _(sp):
                sp.dma_start(w_second[:, :, :], w_out_rows(k, layer, mixer)[:, :, half(1)]).then_inc(w_landed, 16)

            @block.scalar
            def _(act):
                for n in range(NQ):
                    act.wait_ge((k.w_next_landed, w_landed)[n], 16)
                    act.activation(w_hi[:, :, half(n)], w_raw[n], ACT.Copy).then_inc(w_hi_ready, 1)
                    act.activation(y_hi[:, :, half(n)], y[:, :, half(n)], ACT.Copy).then_inc(y_hi_ready, 1)

            @block.gpsimd
            def _(pool):
                for n in range(NQ):
                    pool.wait_ge(w_hi_ready, n + 1)
                    pool.tensor_tensor(w_lo[:, :, half(n)], w_raw[n], w_hi[:, :, half(n)].bitcast(F32),
                                       ALU.subtract).then_inc(w_lo_ready, 1)

            @block.vector
            def _(dve):
                for n in range(NQ):
                    dve.wait_ge(y_hi_ready, n + 1)
                    dve.tensor_tensor(y_lo[:, :, half(n)], y[:, :, half(n)], y_hi[:, :, half(n)].bitcast(F32),
                                      ALU.subtract).then_inc(y_lo_ready, 1)
                for u, (n, t) in enumerate(units):
                    dve.wait_ge(unit_done, u + 1)
                    at = k.x[:, t, half(n)]
                    dve.tensor_tensor(at, at, k.psum[:, u % 8, :], ALU.add).then_inc(added, 1)

            @block.tensor
            def _(pe):
                for u0 in range(0, len(units), TT // NQ):
                    n, half_tok = units[u0][0], units[u0][1] // (TT // NQ)
                    for i, (a, b) in enumerate(((y_hi, w_hi), (y_lo, w_hi), (y_hi, w_lo))):
                        if i == 0:
                            pe.wait_ge(w_hi_ready, n + 1)
                            pe.wait_ge(y_hi_ready, half_tok + 1)
                        elif i == 1:
                            pe.wait_ge(y_lo_ready, half_tok + 1)
                        else:
                            pe.wait_ge(w_lo_ready, n + 1)
                        for u in range(u0, u0 + TT // NQ):
                            t = units[u][1]
                            if i == 0 and u >= 8:
                                pe.wait_ge(added, u - 7)
                            for c in range(CT):
                                last = pe.matmul(k.psum[:, u % 8, :], a[:, c, t * P:(t + 1) * P], b[:, c, half(n)],
                                                 start=(c == 0 and i == 0), stop=(c == CT - 1 and i == 2))
                            if i == 2:
                                last.then_inc(unit_done, 1)
    k.clear(names, fetch_for=layer)


def gate_jobs(sg, mixer, chunks):
    jobs = []
    for i in chunks:
        def evac(eng, ps, mn, i=i):
            m, n = mn
            return eng.activation(sg[:, 2 * i + m, n * BANK:(n + 1) * BANK], ps, ACT.Silu)
        jobs.append((C_GATE + mixer * GROUP_W + i * CHUNK, CHUNK, "C", ("act", evac)))
    return jobs


def gla(k, layer):
    with ExitStack() as outer:
        sg = k.sb(outer, "gla_gate", [P, CT, SEQ])
        gla_inner(k, layer, sg)
        out_block(k, layer, 0, sg, "gla")


def gla_inner(k, layer, sg):
    with ExitStack() as s:
        qT = k.sb(s, "gla_qT", [P, GN, SEQ])
        kT = k.sb(s, "gla_kT", [P, GN, SEQ])
        v = k.sb(s, "gla_v", [P, TT, GROUP_W])
        a_tok = k.sb(s, "gla_a", [P, TT, RANK])

        def c_copy(dst):
            return ("dve", lambda eng, ps, mn: eng.tensor_copy(dst[:, mn[0], mn[1] * BANK:(mn[1] + 1) * BANK], ps))

        def q_copy(eng, ps, mn):
            return eng.tensor_scalar(qT[:, mn[0], mn[1] * BANK:(mn[1] + 1) * BANK], ps, DK ** -0.5, None, ALU.mult)

        def v_copy(eng, ps, t):
            return eng.tensor_copy(v[:, t, 0:CHUNK], ps[:, :CHUNK])

        def v2_copy(eng, ps, t):
            eng.tensor_copy(v[:, t, CHUNK:], ps[:, :CHUNK])
            return eng.tensor_copy(a_tok[:, t, :], ps[:, CHUNK:CHUNK + RANK])

        project_block(k, layer, [
            (C_AQ, CHUNK, "C", ("dve", q_copy)), (C_AK, CHUNK, "C", c_copy(kT)),
            (C_AV, CHUNK, "T", ("dve", v_copy)), (C_AV + CHUNK, CHUNK + RANK, "T", ("dve", v2_copy)),
        ], "gla")

        G = k.sb(s, "gla_G", [P, GN, SEQ])
        gla_decay(k, layer, sg, a_tok, G)
        gla_mix_block(k, layer, qT, kT, v, sg, G)


def gla_decay(k, layer, sg, a_tok, G):
    nc, d = k.nc, k.dram
    names = ["loaded", "transposed", "copied", "product", "biased"]
    loaded, transposed, copied, product, biased = map(k.sem, names)
    side_names = ["logs", "act_chain", "summed"]
    logs, act_chain, summed = map(k.sem, side_names)
    N16 = SEQ // BANK
    with ExitStack() as s2:
        w_up = k.sb(s2, "gla_w_up", [RANK, GN * P])
        b_up = k.sb(s2, "gla_b_up", [P, GN])
        aT = k.sb(s2, "gla_aT", [RANK, SEQ])
        z = G
        e = k.sb(s2, "gla_e", [P, GN, SEQ])
        ones = k.sb(s2, "gla_ones", [P, P])
        with nc.Block() as block:
            @block.sync
            def _(sp):
                sp.dma_start(w_up[:, :], d["gla_w_up"][layer]).then_inc(loaded, 16)
                with nc.allow_non_contiguous_dma(reason="256 biases"):
                    sp.dma_start(b_up[:, :], d["gla_b_up"][layer].rearrange("(g p) -> p g", p=P)).then_inc(loaded, 16)

            @block.tensor
            def _(pe):
                for t in range(TT):
                    last = pe.transpose(k.psum[:RANK, t // 4, (t % 4) * P:(t % 4 + 1) * P], a_tok[:, t, :], k.ident[:, :])
                    if t % 4 == 3:
                        last.then_inc(transposed, 1)
                pe.wait_ge(loaded, 32)
                for g in range(GN):
                    for n in range(N16):
                        pe.wait_ge(copied, n + 1)
                        pe.matmul(k.psum[:, 2 + g * N16 + n, :], w_up[:, g * P:(g + 1) * P],
                                  aT[:, n * BANK:(n + 1) * BANK], start=True, stop=True).then_inc(product, 1)

            @block.vector
            def _(dve):
                dve.memset(ones[:, :], 1.0)
                for n in range(N16):
                    dve.wait_ge(transposed, n + 1)
                    dve.tensor_copy(aT[:, n * BANK:(n + 1) * BANK], k.psum[:RANK, n, :]).then_inc(copied, 1)
                dve.wait_ge(loaded, 32)
                for g in range(GN):
                    for n in range(N16):
                        dve.wait_ge(product, g * N16 + n + 1)
                        dve.tensor_scalar(z[:, g, n * BANK:(n + 1) * BANK], k.psum[:, 2 + g * N16 + n, :],
                                          b_up[:, g:g + 1], None, ALU.add).then_inc(biased, 1)
                dve.wait_ge(biased, GN * N16)
        k.clear(names)

        def scalar(act):
            link = Chain(act, act_chain)
            link(act.activation(e[:, :, :], z[:, :, :], ACT.Abs))
            link(act.activation(e[:, :, :], e[:, :, :], ACT.Exp, scale=-1.0))
            act.activation(e[:, :, :], e[:, :, :], ACT.Ln, bias=1.0).then_inc(logs, 1)

        def vector(dve, _):
            dve.wait_ge(logs, 1)
            dve.scalar_tensor_tensor(out=e[:, :, :], in0=z[:, :, :], scalar=0.0, in1=e[:, :, :],
                                     op0=ALU.min, op1=ALU.subtract).then_inc(summed, 1)
            dve.wait_ge(summed, 1)
            for g in range(GN):
                for t in range(TT):
                    dve.tensor_tensor_scan(G[:, g, t * P:(t + 1) * P], ones[:, :], e[:, g, t * P:(t + 1) * P],
                                           0.0, ALU.mult, ALU.add).then_inc(summed, 1)
            dve.wait_ge(summed, 1 + GN * TT)

        project_block(k, layer, gate_jobs(sg, 0, (0,)), "gla_gate0", side=Side(side_names, scalar, vector))
    project_block(k, layer, gate_jobs(sg, 0, (1,)), "gla_gate1")


def gla_mix_block(k, layer, qT, kT, v, sg, G):
    nc, d = k.nc, k.dram
    names = ["loaded", "exponents", "decays", "q_expanded", "q_level", "q_pool", "k_level", "level_done", "masked",
             "chunk_ends", "k_end_turned", "k_end_copied", "out_done", "state_product", "state_new", "squares",
             "mean", "rstd", "normed", "y_turned", "y_ready", "dve_chain", "act_chain",
             "end_decays"]
    (loaded, exponents, decays, q_expanded, q_level, q_pool, k_level, level_done, masked, chunk_ends, k_end_turned,
     k_end_copied, out_done, state_product, state_new, squares, mean, rstd_ready, normed, y_turned, y_ready,
     dve_chain, act_chain, end_decays) = map(k.sem, names)
    NI = GN + LEVELS
    MIDDLE = GN + 3
    HALF = P // 2
    IN, END = LEVELS, LEVELS + 1
    NB, B_OUT, B_STATE, B_KT, B_Y = 4, 4, 5, 6, 7
    on_pool = (2, 4, 6)
    on_dve = [j for j in range(1, LEVELS + 1) if j not in on_pool]
    RING = 3
    with ExitStack() as s:
        g_out = k.sb(s, "gla_g_out", [P, 1])
        masks = k.sb(s, "gla_masks", [P, LEVELS, HALF], I32)
        E = k.sb(s, "gla_E", [P, 2, LEVELS + 2, GN, P])
        head_mask = k.sb(s, "gla_head_mask", [P, HH])
        q4 = k.sb(s, "gla_q4", [P, GN, HH, P])
        ql = k.sb(s, "gla_ql", [P, RING, GN, HH, HALF])
        kl = k.sb(s, "gla_kl", [P, RING, GN, P])
        k_et = k.sb(s, "gla_k_end_tok", [P, GN * P])
        A = k.sb(s, "gla_A", [P, 2, HEADS, P])
        S = k.sb(s, "gla_S", [P, GN, HH, HEAD])
        to_end = k.sb(s, "gla_to_end", [P, GN, TT])
        end_16 = k.sb(s, "gla_end", [P, GN, TT])
        ms = k.sb(s, "gla_ms", [P, HEADS])
        rstd = k.sb(s, "gla_rstd", [P, HEADS])

        def tok(c):
            return slice(c * P, (c + 1) * P)

        def later(ap, B):
            return ap.rearrange("p g (n h b) -> p g n h b", h=2, b=B)[:, :, :, 1, :]

        def slot_used(m):
            before = m - RING
            return NI * (before // LEVELS) + GN + before % LEVELS + 1

        def expand(eng, c, j, sem):
            B, m = HALF >> (j - 1), LEVELS * c + j - 1
            for g in range(GN):
                e = E[:, c % 2, j - 1, g, :].rearrange("p (n h b) -> p n h b", h=2, b=B)[:, :, 1, :]
                last = eng.tensor_tensor(ql[:, m % RING, g, :, :].rearrange("p h (n b) -> p h n b", b=B),
                                         later(q4[:, g, :, :], B),
                                         e.unsqueeze(1).to_broadcast([P, HH, HALF // B, B]), ALU.mult)
            last.then_inc(sem, 1)

        with nc.Block() as block:
            @block.sync
            def _(sp):
                sp.dma_start(masks[:, :, :], d["c_masks"]).then_inc(loaded, 16)
                sp.dma_start(head_mask[:, :], d["c_head_mask"]).then_inc(loaded, 16)
                with nc.allow_non_contiguous_dma(reason="64 gains"):
                    for i in range(P // HEAD):
                        sp.dma_start(g_out[i * HEAD:(i + 1) * HEAD, :],
                                     d["gla_g_out"][layer].rearrange("(p a) -> p a", a=1)).then_inc(loaded, 16)

            @block.gpsimd
            def _(pool):
                for c in range(TT):
                    pool.wait_ge(decays, c + 1)
                    for j in range(1, LEVELS + 1):
                        m = LEVELS * c + j - 1
                        if m >= RING:
                            pool.wait_ge(level_done, slot_used(m))
                        pool.tensor_tensor(kl[:, m % RING, :, :], kT[:, :, tok(c)], E[:, c % 2, j - 1, :, :], ALU.mult)\
                            .then_inc(k_level, 1)
                        if j in on_pool:
                            if j == on_pool[0]:
                                pool.wait_ge(q_expanded, c + 1)
                            expand(pool, c, j, q_pool)
                    for slot, src in ((IN, qT), (END, kT)):
                        last = pool.tensor_tensor(E[:, c % 2, slot, :, :], src[:, :, tok(c)], E[:, c % 2, slot, :, :],
                                                  ALU.mult)
                    last.then_inc(chunk_ends, 1)

            @block.vector
            def _(dve):
                link = Chain(dve, dve_chain)
                dve.memset(S[:, :, :, :], 0.0).then_inc(state_new, 1)
                dve.wait_ge(state_new, 1)
                dve.wait_ge(loaded, 64)

                def chunk_exponents(c):
                    if c >= 2:
                        dve.wait_ge(k_level, LEVELS * (c - 1))
                        dve.wait_ge(q_pool, len(on_pool) * (c - 1))
                        dve.wait_ge(chunk_ends, c - 1)
                        dve.wait_ge(q_level, len(on_dve) * (c - 1))
                    for j in range(LEVELS):
                        B = 64 >> j
                        gv = G[:, :, tok(c)].rearrange("p g (n h b) -> p g n h b", h=2, b=B)
                        ev = E[:, c % 2, j, :, :].rearrange("p g (n h b) -> p g n h b", h=2, b=B)
                        edge = gv[:, :, :, 0, B - 1:B].to_broadcast([P, GN, 64 // B, B])
                        dve.tensor_tensor(ev[:, :, :, 1, :], gv[:, :, :, 1, :], edge, ALU.subtract)
                        last = dve.tensor_tensor(ev[:, :, :, 0, :], edge, gv[:, :, :, 0, :], ALU.subtract)
                        if j == LEVELS - 1:
                            last.then_inc(exponents, 1)

                def mask(n):
                    c, j = n // NI, n % NI
                    dve.wait_ge(level_done, n + 1)
                    if j < GN:
                        if c >= 2:
                            dve.wait_ge(out_done, c - 1)
                        ps = k.psum[:, n % NB, :].rearrange("p (h t) -> p h t", h=HH)
                        m = k.ident[:, :].unsqueeze(1).to_broadcast([P, HH, P])
                        dve.tensor_tensor(A[:, c % 2, HH * j:HH * (j + 1), :], ps, m, ALU.mult).then_inc(masked, 1)
                    else:
                        B = HALF >> (j - GN)
                        dve.wait_ge(masked, n)
                        ps = k.psum[:, n % NB, :].rearrange("p (h n b) -> p h n b", h=HEADS, b=B)
                        m = masks[:, j - GN, :].rearrange("p (n b) -> p n b", b=B).unsqueeze(1)\
                            .to_broadcast([P, HEADS, HALF // B, B])
                        dve.copy_predicated(later(A[:, c % 2, :, :], B), m, ps).then_inc(masked, 1)

                def products(c, items):
                    for j in items:
                        if j - GN + 1 in on_dve:
                            level = j - GN + 1
                            m = LEVELS * c + level - 1
                            if level == on_dve[0]:
                                dve.wait_ge(q_expanded, c + 1)
                                dve.wait_ge(decays, c + 1)
                            if m >= RING:
                                dve.wait_ge(level_done, slot_used(m))
                            expand(dve, c, level, q_level)
                        if NI * c + j >= 2:
                            mask(NI * c + j - 2)

                def y_evac(c):
                    dve.wait_ge(y_turned, c + 1)
                    at = sg[:, :, tok(c)]
                    dve.scalar_tensor_tensor(out=at, in0=k.psum[:, B_Y, :].rearrange("p (c n) -> p c n", c=CT),
                                             scalar=g_out[:, 0:1], in1=at, op0=ALU.mult, op1=ALU.mult)\
                       .then_inc(y_ready, 1)

                def state(c):
                    dve.wait_ge(state_product, c + 1)
                    dve.wait_ge(end_decays, 1)
                    for g in range(GN):
                        for i in range(HH):
                            r = slice(DK * i, DK * (i + 1))
                            col = g * HALF_W + i * HEAD
                            last = dve.scalar_tensor_tensor(
                                out=S[r, g, i, :], in0=S[r, g, i, :], scalar=to_end[r, g, c:c + 1],
                                in1=k.psum[r, B_STATE, col:col + HEAD], op0=ALU.mult, op1=ALU.add)
                    last.then_inc(state_new, 1)

                def means(c):
                    dve.wait_ge(squares, c + 1)
                    link(dve.tensor_reduce(ms[:, :], v[:, c, :].rearrange("p (h e) -> p h e", e=HEAD), AX_X, ALU.add))
                    dve.tensor_scalar(ms[:, :], ms[:, :], 1.0 / HEAD, EPS, ALU.mult, ALU.add).then_inc(mean, 1)

                def normalise(c):
                    dve.wait_ge(rstd_ready, c + 1)
                    dve.tensor_tensor(v[:, c, :].rearrange("p (h e) -> p h e", e=HEAD),
                                      k.psum[:, B_OUT, :].rearrange("p (h e) -> p h e", e=HEAD),
                                      head_bcast(rstd[:, :], HEAD), ALU.mult).then_inc(normed, 1)

                chunk_exponents(0)
                for c in range(TT + 1):
                    if c < TT:
                        products(c, range(MIDDLE))
                    else:
                        mask(NI * TT - 2)
                        mask(NI * TT - 1)
                    if c >= 2:
                        y_evac(c - 2)
                    if c + 1 < TT:
                        chunk_exponents(c + 1)
                    if 1 <= c < TT:
                        state(c - 1)
                    if c >= 1:
                        means(c - 1)
                    if c < TT:
                        products(c, range(MIDDLE, NI))
                    if c >= 1:
                        normalise(c - 1)
                y_evac(TT - 1)

            @block.scalar
            def _(act):
                link = Chain(act, act_chain)

                def expand_q(c):
                    if c >= 1:
                        act.wait_ge(level_done, NI * (c - 1) + GN)
                        act.wait_ge(q_pool, len(on_pool) * c)
                        act.wait_ge(q_level, len(on_dve) * c)
                    for i in range(HH):
                        last = act.activation(q4[:, :, i, :], qT[:, :, tok(c)], ACT.Copy, scale=head_mask[:, i:i + 1])
                    last.then_inc(q_expanded, 1)

                def decay(c):
                    act.wait_ge(exponents, c + 1)
                    at = E[:, c % 2, :LEVELS, :, :]
                    act.activation(at, at, ACT.Exp, scale=1.0 / 16.0)
                    act.activation(E[:, c % 2, IN, :, :], G[:, :, tok(c)], ACT.Exp, scale=1.0 / 16.0)
                    for g in range(GN):
                        last = act.activation(E[:, c % 2, END, g, :], G[:, g, tok(c)], ACT.Exp, scale=-1.0 / 16.0,
                                              bias=end_16[:, g, c:c + 1])
                    last.then_inc(decays, 1)

                link(act.activation(end_16[:, :, :], G[:, :, P - 1::P], ACT.Copy, scale=1.0 / 16.0))
                act.wait_ge(loaded, 64)
                expand_q(0)
                decay(0)
                act.activation(to_end[:, :, :], G[:, :, P - 1::P], ACT.Exp, scale=1.0 / 16.0).then_inc(end_decays, 1)
                for c in range(TT + 1):
                    if c >= 1:
                        act.wait_ge(k_end_turned, c)
                        act.activation(k_et[:, :], k.psum[:, B_KT, :GN * P], ACT.Copy).then_inc(k_end_copied, 1)
                        act.wait_ge(out_done, c)
                        if c < TT:
                            act.wait_ge(state_product, c)
                        act.activation(v[:, c - 1, :], k.psum[:, B_OUT, :], ACT.Square).then_inc(squares, 1)
                    if c + 1 < TT:
                        decay(c + 1)
                    if c >= 1:
                        act.wait_ge(mean, c)
                        link(act.activation(rstd[:, :], ms[:, :], ACT.Ln))
                        act.activation(rstd[:, :], rstd[:, :], ACT.Exp, scale=-0.5).then_inc(rstd_ready, 1)
                    if c + 1 < TT:
                        expand_q(c + 1)

            @block.tensor
            def _(pe):
                def products(c, items):
                    for j in items:
                        n = NI * c + j
                        if n >= NB:
                            pe.wait_ge(masked, n - NB + 1)
                        if j < GN:
                            pe.wait_ge(q_expanded, c + 1)
                            last = pe.matmul(k.psum[:, n % NB, :], kT[:, j, tok(c)],
                                             q4[:, j, :, :].rearrange("p h t -> p (h t)"), start=True, stop=True)
                        else:
                            level = j - GN + 1
                            m = LEVELS * c + level - 1
                            pe.wait_ge(k_level, m + 1)
                            if level in on_pool:
                                pe.wait_ge(q_pool, len(on_pool) * c + on_pool.index(level) + 1)
                            else:
                                pe.wait_ge(q_level, len(on_dve) * c + on_dve.index(level) + 1)
                            for g in range(GN):
                                last = pe.matmul(k.psum[:, n % NB, g * HH * HALF:(g + 1) * HH * HALF],
                                                 kl[:, m % RING, g, :], ql[:, m % RING, g, :, :]
                                                 .rearrange("p h t -> p (h t)"), start=True, stop=True)
                        last.then_inc(level_done, 1)

                def finish(c):
                    pe.wait_ge(chunk_ends, c + 1)
                    if c >= 1:
                        pe.wait_ge(k_end_copied, c)
                        pe.wait_ge(normed, c)
                    for g in range(GN):
                        last = pe.transpose(k.psum[:, B_KT, g * P:(g + 1) * P], E[:, c % 2, END, g, :], k.ident[:, :])
                    last.then_inc(k_end_turned, 1)
                    pe.wait_ge(masked, NI * (c + 1))
                    pe.wait_ge(state_new, c + 1)
                    for g in range(GN):
                        o = k.psum[:, B_OUT, g * HALF_W:(g + 1) * HALF_W]
                        pe.matmul(o, E[:, c % 2, IN, g, :], S[:, g, :, :].rearrange("p h e -> p (h e)"), start=True, stop=False,
                                  skip_group_check=True)
                        for i in range(HH):
                            last = pe.matmul(o[:, i * HEAD:(i + 1) * HEAD], A[:, c % 2, HH * g + i, :],
                                             v[:, c, g * HALF_W + i * HEAD:g * HALF_W + (i + 1) * HEAD],
                                             start=False, stop=(i == HH - 1), skip_group_check=True)
                    last.then_inc(out_done, 1)
                    if c < TT - 1:
                        pe.wait_ge(k_end_copied, c + 1)
                        for g in range(GN):
                            last = pe.matmul(k.psum[:, B_STATE, g * HALF_W:(g + 1) * HALF_W], k_et[:, g * P:(g + 1) * P],
                                             v[:, c, g * HALF_W:(g + 1) * HALF_W], start=True, stop=True)
                        last.then_inc(state_product, 1)

                def turn_y(c):
                    pe.wait_ge(normed, c + 1)
                    if c >= 1:
                        pe.wait_ge(y_ready, c)
                    for i in range(CT):
                        last = pe.transpose(k.psum[:, B_Y, i * P:(i + 1) * P], v[:, c, i * P:(i + 1) * P], k.ident[:, :])
                    last.then_inc(y_turned, 1)

                warm_clock(k, pe, B_Y)
                for c in range(TT + 1):
                    if c < TT:
                        products(c, range(MIDDLE))
                    if c >= 1:
                        finish(c - 1)
                    if c < TT:
                        products(c, range(MIDDLE, NI))
                    if c >= 1:
                        turn_y(c - 1)
    k.clear(names)


def turn_block(k, q, kk, qT, kT, q_gain, k_gain, width):
    nc = k.nc
    names = ["q_turned", "k_turned", "q_evac", "k_evac"]
    q_turned, k_turned, q_evac, k_evac = map(k.sem, names)
    RING = 4
    with nc.Block() as block:
        @block.tensor
        def _(pe):
            for t in range(TT):
                for src, bank, turned, evac in ((q, 0, q_turned, q_evac), (kk, RING, k_turned, k_evac)):
                    if t >= RING:
                        pe.wait_ge(evac, t - RING + 1)
                    for h in range(HH):
                        last = pe.transpose(k.psum[:width, bank + t % RING, h * P:(h + 1) * P], src[:, t, h, :],
                                            k.ident[:, :])
                    last.then_inc(turned, 1)

        @block.scalar
        def _(act):
            for t in range(TT):
                act.wait_ge(q_turned, t + 1)
                src = k.psum[:width, t % RING, :].rearrange("p (h n) -> p h n", h=HH)
                act.activation(qT[:, :, t * P:(t + 1) * P], src, ACT.Copy, scale=q_gain[:, 0:1]).then_inc(q_evac, 1)

        @block.vector
        def _(dve):
            for t in range(TT):
                dve.wait_ge(k_turned, t + 1)
                src = k.psum[:width, RING + t % RING, :].rearrange("p (h n) -> p h n", h=HH)
                dve.tensor_scalar(kT[:, :, t * P:(t + 1) * P], src, k_gain[:, 0:1], None, ALU.mult)\
                   .then_inc(k_evac, 1)
    k.clear(names)


def attention_block(k, qT, kT, v, sg, p_buf, pt_buf, tag):
    nc = k.nc
    names = ["scores", "max_done", "probs", "p_turned", "pt_dve", "pt_act", "pv_done", "normed", "y_turned",
             "y_ready", "dve_chain"]
    (scores, max_done, probs, p_turned, pt_dve, pt_act, pv_done, normed, y_turned, y_ready,
     dve_chain) = map(k.sem, names)
    U = TT * HH
    B_PT, B_O, GROUP = 4, 6, 4
    groups = [(u, g) for u in range(U) for g in range((u // HH) // GROUP + 1)]
    first = {u: groups.index((u, 0)) for u in range(U)}
    by = ["act" if g % 2 else "dve" for _, g in groups]
    nth = [by[:i + 1].count(by[i]) for i in range(len(groups))]
    pt_sem = {"dve": pt_dve, "act": pt_act}

    def blocks(u, g):
        return range(g * GROUP, min((g + 1) * GROUP, u // HH + 1))

    def group_list(u):
        return [(first[u] + g, blocks(u, g)) for g in range((u // HH) // GROUP + 1)]

    def score_ap(u):
        b = 2 * (u % 2)
        return k.psum[:, b:b + 2, :].rearrange("p b n -> p (b n)")[:, :(u // HH + 1) * P]

    with ExitStack() as s:
        nmax = k.sb(s, tag + "_nmax", [P, U])
        rsum = k.sb(s, tag + "_rsum", [P, U])
        rinv = k.sb(s, tag + "_rinv", [P, U])
        on = k.sb(s, tag + "_on", [P, HALF_W])
        p_sb = p_buf[:, :2 * SEQ].rearrange("p (a n) -> p a n", a=2)
        pt_sb = pt_buf[:, :2 * SEQ].rearrange("p (a n) -> p a n", a=2)

        def copy_pt(eng, me, u, op):
            for i, bl in group_list(u):
                if by[i] == me:
                    eng.wait_ge(p_turned, i + 1)
                    if u >= 2:
                        eng.wait_ge(pv_done, u - 1)
                    op(pt_sb[:, u % 2, bl[0] * P:(bl[-1] + 1) * P], k.psum[:, B_PT + i % 2, :len(bl) * P])\
                        .then_inc(pt_sem[me], 1)

        with nc.Block() as block:
            @block.tensor
            def _(pe):
                def score(u):
                    qt, h = u // HH, u % HH
                    if u >= 2:
                        pe.wait_ge(probs, u - 1)
                    out, n = score_ap(u), (qt + 1) * P
                    for c0 in range(0, n, BANK):
                        c1 = min(c0 + BANK, n)
                        pe.matmul(out[:, c0:c1], qT[:, h, qt * P:(qt + 1) * P], kT[:, h, c0:c1], start=True,
                                  stop=(c1 < n))
                    pe.matmul(out[:, qt * P:n], k.ident_bf[:, :], k.mask_bf[:, :], start=False, stop=True)\
                      .then_inc(scores, 1)

                def turn(u):
                    pe.wait_ge(probs, u + 1)
                    for i, bl in group_list(u):
                        if i >= 2:
                            pe.wait_ge(pt_sem[by[i - 2]], nth[i - 2])
                        for j, b in enumerate(bl):
                            last = pe.transpose(k.psum[:, B_PT + i % 2, j * P:(j + 1) * P],
                                                p_sb[:, u % 2, b * P:(b + 1) * P], k.ident[:, :])
                        last.then_inc(p_turned, 1)

                def pv(u):
                    qt, h = u // HH, u % HH
                    if h == 0 and qt >= 2:
                        pe.wait_ge(y_ready, qt - 1)
                    for i, bl in group_list(u):
                        pe.wait_ge(pt_sem[by[i]], nth[i])
                        for b in bl:
                            last = pe.matmul(k.psum[:, B_O + qt % 2, h * HEAD:(h + 1) * HEAD],
                                             pt_sb[:, u % 2, b * P:(b + 1) * P], v[:, b, h * HEAD:(h + 1) * HEAD],
                                             start=(b == 0), stop=(b == qt))
                    last.then_inc(pv_done, 1)

                def turn_y(qt):
                    pe.wait_ge(normed, qt + 1)
                    for i in range(HALF_W // P):
                        last = pe.transpose(k.psum[:, B_O + qt % 2, HALF_W + i * P:HALF_W + (i + 1) * P],
                                            on[:, i * P:(i + 1) * P], k.ident[:, :])
                    last.then_inc(y_turned, 1)

                warm_clock(k, pe, B_O + 1)
                for u in range(U + 2):
                    if u < U:
                        score(u)
                    if 1 <= u <= U:
                        turn(u - 1)
                    if u >= 2:
                        pv(u - 2)
                        if (u - 2) % HH == 1 and u - 2 > HH:
                            turn_y((u - 2) // HH - 1)
                turn_y(TT - 1)

            @block.vector
            def _(dve):
                link = Chain(dve, dve_chain)

                def normalise(qt):
                    dve.wait_ge(pv_done, HH * (qt + 1))
                    if qt >= 1:
                        dve.wait_ge(y_turned, qt)
                    cols = slice(HH * qt, HH * (qt + 1))
                    link(dve.reciprocal(rinv[:, cols], rsum[:, cols]))
                    dve.tensor_tensor(on[:, :].rearrange("p (h e) -> p h e", e=HEAD),
                                      k.psum[:, B_O + qt % 2, :HALF_W].rearrange("p (h e) -> p h e", e=HEAD),
                                      head_bcast(rinv[:, cols], HEAD), ALU.mult).then_inc(normed, 1)

                def y_evac(qt):
                    dve.wait_ge(y_turned, qt + 1)
                    at = sg[:, :, qt * P:(qt + 1) * P]
                    dve.tensor_tensor(at, k.psum[:, B_O + qt % 2, HALF_W:].rearrange("p (c n) -> p c n", n=P), at,
                                      ALU.mult).then_inc(y_ready, 1)

                for u in range(U + 1):
                    if u < U:
                        dve.wait_ge(scores, u + 1)
                        dve.tensor_reduce(nmax[:, u:u + 1], score_ap(u), AX_X, ALU.max, negate=True)\
                           .then_inc(max_done, 1)
                    if u >= 1:
                        copy_pt(dve, "dve", u - 1, dve.tensor_copy)
                    if u % HH == 2 and u > HH:
                        normalise(u // HH - 1)
                    if u % HH == 3 and u > HH:
                        y_evac(u // HH - 1)
                normalise(TT - 1)
                y_evac(TT - 1)

            @block.scalar
            def _(act):
                for u in range(U + 1):
                    if u < U:
                        act.wait_ge(max_done, u + 1)
                        if u >= 2:
                            act.wait_ge(p_turned, first[u - 1])
                        n = (u // HH + 1) * P
                        act.activation(p_sb[:, u % 2, :n], score_ap(u), ACT.Exp, bias=nmax[:, u:u + 1],
                                       accum_out=rsum[:, u:u + 1]).then_inc(probs, 1)
                    if u >= 1:
                        copy_pt(act, "act", u - 1, lambda o, i: act.activation(o, i, ACT.Copy))
    k.clear(names)


def fox(k, layer):
    nc, d = k.nc, k.dram
    with ExitStack() as s:
        sg = k.sb(s, "fox_gate", [P, CT, SEQ])
        cum = k.sb(s, "fox_cum", [P, 2, TT, HEADS])
        f_tok = k.sb(s, "fox_f", [P, TT, HEADS])
        q_gain = k.sb(s, "fox_q_gain", [FOX_D, 1])
        k_gain = k.sb(s, "fox_k_gain", [FOX_D, 1])
        for half in (1, 0):
            with ExitStack() as s2:
                v = k.sb(s2, "fox_v", [P, TT, HALF_W])
                qa = k.sb(s2, "fox_qa", [P, TT, HH, FOX_D])
                ka = k.sb(s2, "fox_ka", [P, TT, HH, FOX_D])

                def to_v(eng, ps, t):
                    return eng.tensor_copy(v[:, t, :], ps[:, :HALF_W])

                def to(dst):
                    return ("dve", lambda eng, ps, t: eng.tensor_copy(
                        dst[:, t, :, :HEAD], ps[:, :HALF_W].rearrange("p (h e) -> p h e", e=HEAD)))

                def v_and_f(eng, ps, t):
                    eng.tensor_copy(v[:, t, :], ps[:, :HALF_W])
                    return eng.tensor_copy(f_tok[:, t, :], ps[:, HALF_W:HALF_W + HEADS])

                off = half * HALF_W
                jobs = [(C_BQ + off, HALF_W, "T", to(qa)), (C_BK + off, HALF_W, "T", to(ka))]
                if half == 1:
                    jobs += [(C_BV + off, HALF_W + HEADS, "T", ("dve", v_and_f))]
                else:
                    jobs += [(C_BV + off, HALF_W, "T", ("dve", to_v))]
                project_block(k, layer, jobs, "fox")
                if half == 1:
                    forget_block(k, layer, f_tok, cum, q_gain, k_gain)
                with ExitStack() as s3:
                    project_block(k, layer, gate_jobs(sg, 1, (half,)), "fox",
                                  side=fox_norm_side(k, s3, qa, ka, cum, half))
                qT = k.sb(s2, "fox_qT", [FOX_D, HH, SEQ])
                kT = k.sb(s2, "fox_kT", [FOX_D, HH, SEQ])
                turn_block(k, qa, ka, qT, kT, q_gain, k_gain, FOX_D)
                attention_block(k, qT, kT, v, sg[:, 2 * half:2 * half + 2, :],
                                qa[:, :, :, :].rearrange("p t h e -> p (t h e)"),
                                ka[:, :, :, :].rearrange("p t h e -> p (t h e)"), "fox")
        out_block(k, layer, 1, sg, "fox")


def forget_block(k, layer, f_tok, cum, q_gain, k_gain):
    nc, d = k.nc, k.dram
    names = ["loaded", "dve_chain", "handover", "logs", "act_chain", "product"]
    loaded, dve_chain, handover, logs, act_chain, product = map(k.sem, names)
    with ExitStack() as s:
        bias = k.sb(s, "fox_b", [P, HEADS])
        upper = k.sb(s, "fox_upper", [P, P])
        ones = k.sb(s, "fox_ones", [P, P])
        z = k.sb(s, "fox_z", [P, TT, HEADS])
        az = k.sb(s, "fox_az", [P, TT, HEADS])
        ls = k.sb(s, "fox_ls", [P, TT, HEADS])
        before = k.sb(s, "fox_before", [P, TT, HEADS])
        flat = "p t h -> p (t h)"
        with nc.Block() as block:
            @block.sync
            def _(sp):
                sp.dma_start(bias[:, :], bcast_rows(d["fox_b_f"][layer], P)).then_inc(loaded, 16)
                sp.dma_start(upper[:, :], d["c_upper"]).then_inc(loaded, 16)
                for g, name in ((q_gain, "fox_g_q"), (k_gain, "fox_g_k")):
                    with nc.allow_non_contiguous_dma(reason="64 gains"):
                        sp.dma_start(g[:HEAD, :], d[name][layer].rearrange("(p a) -> p a", a=1)).then_inc(loaded, 16)

            @block.vector
            def _(dve):
                link = Chain(dve, dve_chain)
                dve.memset(q_gain[HEAD:FOX_D, :], 1.0)
                dve.memset(k_gain[HEAD:FOX_D, :], 1.0)
                dve.memset(ones[:, :], 1.0)
                dve.wait_ge(loaded, 64)
                dve.tensor_scalar(q_gain[:HEAD, :], q_gain[:HEAD, :], HEAD ** -0.5, None, ALU.mult)
                link(dve.tensor_tensor(z[:, :, :], f_tok[:, :, :], bias[:, :].unsqueeze(1).to_broadcast([P, TT, HEADS]),
                                       ALU.add))
                link(dve.tensor_scalar(az[:, :, :], z[:, :, :], -1.0, None, ALU.mult))
                dve.tensor_tensor(az[:, :, :], az[:, :, :], z[:, :, :], ALU.max).then_inc(handover, 1)
                dve.wait_ge(logs, 1)
                link(dve.scalar_tensor_tensor(out=ls[:, :, :], in0=z[:, :, :], scalar=0.0, in1=az[:, :, :],
                                              op0=ALU.min, op1=ALU.subtract))
                link(dve.memset(before[:, 0, :], 0.0))
                for t in range(1, TT):
                    link(dve.tensor_tensor(before[:, t, :], before[:, t - 1, :], ls[:, t - 1, :], ALU.add))
                dve.sem_inc(handover, 1)
                dve.wait_ge(product, 1)
                dve.tensor_copy(cum[:, 0, :, :].rearrange(flat), k.psum[:, 0, :TT * HEADS])
                link(dve.tensor_scalar(cum[:, 1, :, :].rearrange(flat), k.psum[:, 0, :TT * HEADS], -1.0, None, ALU.mult))

            @block.scalar
            def _(act):
                link = Chain(act, act_chain)
                act.wait_ge(handover, 1)
                link(act.activation(az[:, :, :], az[:, :, :], ACT.Exp, scale=-1.0))
                act.activation(az[:, :, :], az[:, :, :], ACT.Ln, bias=1.0).then_inc(logs, 1)

            @block.tensor
            def _(pe):
                pe.wait_ge(handover, 2)
                pe.matmul(k.psum[:, 0, :TT * HEADS], upper[:, :], ls[:, :, :].rearrange(flat), start=True, stop=False)
                pe.matmul(k.psum[:, 0, :TT * HEADS], ones[:, :], before[:, :, :].rearrange(flat), start=False,
                          stop=True).then_inc(product, 1)
    k.clear(names)


def fox_norm_side(k, s, qa, ka, cum, half):
    names = ["squares", "mean", "rstd", "act_chain", "dve_chain"]
    squares, mean, rstd_ready, act_chain, dve_chain = map(k.sem, names)
    N = TT * HH
    sq = k.sb(s, "fox_sq", [P, N, HEAD])
    ms = k.sb(s, "fox_ms", [P, 2, N])

    def heads(x):
        return x[:, :, :, :].rearrange("p t h e -> p (t h) e")[:, :, :HEAD]

    def scalar(act):
        link = Chain(act, act_chain)
        for i, x in enumerate((qa, ka)):
            if i:
                act.wait_ge(mean, i)
            act.activation(sq[:, :, :], heads(x), ACT.Square).then_inc(squares, 1)
        act.wait_ge(mean, 2)
        link(act.activation(ms[:, :, :], ms[:, :, :], ACT.Ln))
        act.activation(ms[:, :, :], ms[:, :, :], ACT.Exp, scale=-0.5).then_inc(rstd_ready, 1)

    def vector(dve, _):
        link = Chain(dve, dve_chain)
        for i in range(2):
            dve.wait_ge(squares, i + 1)
            link(dve.tensor_reduce(ms[:, i, :], sq[:, :, :], AX_X, ALU.add))
            dve.tensor_scalar(ms[:, i, :], ms[:, i, :], 1.0 / HEAD, EPS, ALU.mult, ALU.add).then_inc(mean, 1)
        hs = slice(half * HH, (half + 1) * HH)
        dve.memset(qa[:, :, :, HEAD + 1:], 1.0)
        dve.memset(ka[:, :, :, HEAD:HEAD + 1], 1.0)
        dve.tensor_copy(qa[:, :, :, HEAD], cum[:, 0, :, hs])
        dve.tensor_copy(ka[:, :, :, HEAD + 1], cum[:, 1, :, hs])
        dve.wait_ge(rstd_ready, 1)
        for i, x in enumerate((qa, ka)):
            link(dve.tensor_tensor(heads(x), heads(x), head_bcast(ms[:, i, :], HEAD), ALU.mult))

    return Side(names, scalar, vector)


def rope(dve, link, cos, sin, src, dst, tmp):
    HR = ROPE // 2
    lead = (slice(None),) * (len(src.shape) - 1)
    z1, z2 = src[lead + (slice(0, HR),)], src[lead + (slice(HR, ROPE),)]
    o1, o2 = dst[lead + (slice(0, HR),)], dst[lead + (slice(HR, ROPE),)]
    a, b, c, e = tmp
    dve.tensor_tensor(a, z1, cos, ALU.mult)
    dve.tensor_tensor(b, z2, sin, ALU.mult)
    dve.tensor_tensor(c, z1, sin, ALU.mult)
    link(dve.tensor_tensor(e, z2, cos, ALU.mult))
    dve.tensor_tensor(o1, a, b, ALU.subtract)
    link(dve.tensor_tensor(o2, c, e, ALU.add))


def mla(k, layer):
    with ExitStack() as outer:
        sg = k.sb(outer, "mla_gate", [P, CT, SEQ])
        mla_inner(k, layer, sg)
        out_block(k, layer, 2, sg, "mla")


def mla_inner(k, layer, sg):
    with ExitStack() as s:
        cqT = k.sb(s, "mla_cqT", [P, Q_RANK // P, SEQ])
        ckvT = k.sb(s, "mla_ckvT", [P, SEQ])
        kr = k.sb(s, "mla_kr", [P, TT, ROPE])
        kr_rot = k.sb(s, "mla_kr_rot", [P, TT, ROPE])
        q_gain = k.sb(s, "mla_q_gain", [MLA_D, 1])
        k_gain = k.sb(s, "mla_k_gain", [MLA_D, 1])
        rope_gain = k.sb(s, "mla_rope_gain", [P, 2, ROPE])
        with ExitStack() as s2:
            lat = k.sb(s2, "mla_lat", [P, TT, Q_RANK + KV_RANK])

            def to_q(eng, ps, t):
                return eng.tensor_copy(lat[:, t, :Q_RANK], ps[:, :Q_RANK])

            def to_kv(eng, ps, t):
                eng.tensor_copy(lat[:, t, Q_RANK:], ps[:, :KV_RANK])
                return eng.tensor_copy(kr[:, t, :], ps[:, KV_RANK:KV_RANK + ROPE])

            project_block(k, layer, [(C_CQ, Q_RANK, "T", ("dve", to_q)),
                                     (C_CKV, KV_RANK + ROPE, "T", ("dve", to_kv))], "mla")
            latent_block(k, layer, s2, lat, cqT, ckvT, kr, kr_rot, q_gain, k_gain, rope_gain)
        for half in range(2):
            with ExitStack() as s2:
                v = k.sb(s2, "mla_v", [P, TT, HALF_W])
                q_raw = k.sb(s2, "mla_q", [P, TT, HH, MLA_D])
                k_raw = k.sb(s2, "mla_k", [P, TT, HH, MLA_D])
                expand_block(k, layer, half, cqT, ckvT, kr, v, q_raw, k_raw)
                with ExitStack() as s3:
                    project_block(k, layer, gate_jobs(sg, 2, (half,)), "mla",
                                  side=mla_norm_side(k, s3, kr_rot, rope_gain, q_raw, k_raw))
                qT = k.sb(s2, "mla_qT", [MLA_D, HH, SEQ])
                kT = k.sb(s2, "mla_kT", [MLA_D, HH, SEQ])
                turn_block(k, q_raw, k_raw, qT, kT, q_gain, k_gain, MLA_D)
                attention_block(k, qT, kT, v, sg[:, 2 * half:2 * half + 2, :],
                                q_raw[:, :, :, :].rearrange("p t h e -> p (t h e)"),
                                k_raw[:, :, :, :].rearrange("p t h e -> p (t h e)"), "mla")


def latent_block(k, layer, s, lat, cqT, ckvT, kr, kr_rot, q_gain, k_gain, rope_gain):
    nc, d = k.nc, k.dram
    names = ["loaded", "squares", "mean", "rstd", "normed", "turned", "evac", "dve_chain", "act_chain"]
    loaded, squares, mean, rstd_ready, normed, turned, evac, dve_chain, act_chain = map(k.sem, names)
    W = Q_RANK + KV_RANK
    NC = W // P
    gain = k.sb(s, "mla_lat_gain", [P, W])
    sq = k.sb(s, "mla_lat_sq", [P, TT, W])
    ms = k.sb(s, "mla_lat_ms", [P, 2, TT])
    krg = k.sb(s, "mla_krg", [P, TT, ROPE])
    tmp = [k.sb(s, f"mla_kr_tmp{i}", [P, TT, ROPE // 2]) for i in range(4)]
    parts = ((0, Q_RANK), (Q_RANK, W))
    with nc.Block() as block:
        @block.sync
        def _(sp):
            sp.dma_start(gain[:, :Q_RANK], bcast_rows(d["mla_g_cq"][layer], P)).then_inc(loaded, 16)
            sp.dma_start(gain[:, Q_RANK:], bcast_rows(d["mla_g_ckv"][layer], P)).then_inc(loaded, 16)
            for i, (g, name) in enumerate(((q_gain, "mla_g_q"), (k_gain, "mla_g_k"))):
                with nc.allow_non_contiguous_dma(reason="64 gains"):
                    sp.dma_start(g[:HEAD, :], d[name][layer, 0:HEAD].rearrange("(p a) -> p a", a=1)).then_inc(loaded, 16)
                sp.dma_start(rope_gain[:, i, :], bcast_rows(d[name][layer, HEAD:MLA_D], P)).then_inc(loaded, 16)

        @block.scalar
        def _(act):
            link = Chain(act, act_chain)
            act.activation(sq[:, :, :], lat[:, :, :], ACT.Square).then_inc(squares, 1)
            act.wait_ge(mean, 1)
            link(act.activation(ms[:, :, :], ms[:, :, :], ACT.Ln))
            act.activation(ms[:, :, :], ms[:, :, :], ACT.Exp, scale=-0.5).then_inc(rstd_ready, 1)
            for t in range(TT):
                act.wait_ge(turned, t + 1)
                tok = slice(t * P, (t + 1) * P)
                src = k.psum[:, t, :W].rearrange("p (c n) -> p c n", n=P)
                act.activation(cqT[:, :, tok], src[:, :Q_RANK // P, :], ACT.Copy).then_inc(evac, 1)
                act.activation(ckvT[:, tok], src[:, Q_RANK // P, :], ACT.Copy).then_inc(evac, 1)
            act.wait_ge(evac, 2 * TT)

        @block.vector
        def _(dve):
            link = Chain(dve, dve_chain)
            dve.memset(q_gain[HEAD:, :], 1.0)
            link(dve.memset(k_gain[HEAD:, :], 1.0))
            dve.wait_ge(squares, 1)
            for i, (a, b) in enumerate(parts):
                link(dve.tensor_reduce(ms[:, i, :], sq[:, :, a:b], AX_X, ALU.add))
                last = dve.tensor_scalar(ms[:, i, :], ms[:, i, :], 1.0 / (b - a), EPS, ALU.mult, ALU.add)
            last.then_inc(mean, 1)
            dve.wait_ge(loaded, 96)
            dve.wait_ge(rstd_ready, 1)
            for t in range(TT):
                for i, (a, b) in enumerate(parts):
                    last = dve.scalar_tensor_tensor(out=lat[:, t, a:b], in0=lat[:, t, a:b], scalar=ms[:, i, t:t + 1],
                                                    in1=gain[:, a:b], op0=ALU.mult, op1=ALU.mult)
                last.then_inc(normed, 1)
            link(dve.tensor_scalar(q_gain[:, :], q_gain[:, :], MLA_D ** -0.5, None, ALU.mult))
            link(dve.tensor_tensor(krg[:, :, :], kr[:, :, :], rope_gain[:, 1, :].unsqueeze(1).to_broadcast([P, TT, ROPE]),
                                   ALU.mult))
            rope(dve, link, k.cos[:, :, :], k.sin[:, :, :], krg[:, :, :], kr_rot[:, :, :], [x[:, :, :] for x in tmp])

        @block.tensor
        def _(pe):
            for t in range(TT):
                pe.wait_ge(normed, t + 1)
                for c in range(NC):
                    last = pe.transpose(k.psum[:, t, c * P:(c + 1) * P], lat[:, t, c * P:(c + 1) * P], k.ident[:, :])
                last.then_inc(turned, 1)
    k.clear(names)


def expand_block(k, layer, half, cqT, ckvT, kr, v, q_raw, k_raw):
    nc, d = k.nc, k.dram
    names = ["loaded", "q_product", "kv_product", "q_evac", "kv_evac"]
    loaded, q_product, kv_product, q_evac, kv_evac = map(k.sem, names)
    QW, KVW = HH * MLA_D, HH * 2 * HEAD
    NQ = Q_RANK // P
    with ExitStack() as s:
        w_uq = k.sb(s, "mla_w_uq", [P, NQ, QW])
        w_ukv = k.sb(s, "mla_w_ukv", [P, KVW])
        with nc.Block() as block:
            @block.sync
            def _(sp):
                sp.dma_start(w_uq[:, :, :], d["mla_w_uq"][layer].rearrange("(c p) n -> p c n", p=P)
                             [:, :, half * QW:(half + 1) * QW]).then_inc(loaded, 16)
                sp.dma_start(w_ukv[:, :], d["mla_w_ukv"][layer][:, half * KVW:(half + 1) * KVW]).then_inc(loaded, 16)

            @block.tensor
            def _(pe):
                pe.wait_ge(loaded, 32)
                for t in range(TT):
                    tok = slice(t * P, (t + 1) * P)
                    if t >= 4:
                        pe.wait_ge(q_evac, t - 3)
                        pe.wait_ge(kv_evac, t - 3)
                    for c in range(NQ):
                        last = pe.matmul(k.psum[:, t % 4, :QW], cqT[:, c, tok], w_uq[:, c, :], start=(c == 0),
                                         stop=(c == NQ - 1))
                    last.then_inc(q_product, 1)
                    pe.matmul(k.psum[:, 4 + t % 4, :KVW], ckvT[:, tok], w_ukv[:, :], start=True, stop=True)\
                      .then_inc(kv_product, 1)

            @block.scalar
            def _(act):
                for t in range(TT):
                    act.wait_ge(q_product, t + 1)
                    act.activation(q_raw[:, t, :, :].rearrange("p h e -> p (h e)"), k.psum[:, t % 4, :QW], ACT.Copy)\
                       .then_inc(q_evac, 1)
                act.wait_ge(q_evac, TT)

            @block.vector
            def _(dve):
                for t in range(TT):
                    dve.wait_ge(kv_product, t + 1)
                    src = k.psum[:, 4 + t % 4, :].rearrange("p (h e) -> p h e", h=HH)
                    dve.tensor_copy(k_raw[:, t, :, :HEAD], src[:, :, :HEAD])
                    dve.tensor_copy(v[:, t, :].rearrange("p (h e) -> p h e", h=HH), src[:, :, HEAD:]).then_inc(kv_evac, 1)
                dve.tensor_copy(k_raw[:, :, :, HEAD:], kr[:, :, :].unsqueeze(2).to_broadcast([P, TT, HH, ROPE]))\
                   .then_inc(kv_evac, 1)
                dve.wait_ge(kv_evac, TT + 1)
    k.clear(names)


def mla_norm_side(k, s, kr_rot, rope_gain, q_raw, k_raw):
    names = ["squares", "mean", "rstd", "dve_chain", "act_chain"]
    squares, mean, rstd_ready, dve_chain, act_chain = map(k.sem, names)
    N, HR = TT * HH, ROPE // 2
    NS = 4
    sq = k.sb(s, "mla_sq", [P, 2048])
    ms = k.sb(s, "mla_ms", [P, NS, N // 2])
    sq_v = sq[:, :N // 2 * MLA_D].rearrange("p (n e) -> p n e", e=MLA_D)
    tmp = [sq[:, i * N * HR:(i + 1) * N * HR].rearrange("p (t h e) -> p t h e", t=TT, h=HH) for i in range(4)]
    q_all = q_raw[:, :, :, :].rearrange("p t h e -> p (t h) e")
    k_all = k_raw[:, :, :, :].rearrange("p t h e -> p (t h) e")
    parts = [x[:, i * N // 2:(i + 1) * N // 2, :] for x in (q_all, k_all) for i in range(2)]

    def scalar(act):
        link = Chain(act, act_chain)
        for i, x in enumerate(parts):
            if i:
                act.wait_ge(mean, i)
            act.activation(sq_v, x, ACT.Square).then_inc(squares, 1)
        act.wait_ge(mean, NS)
        link(act.activation(ms[:, :, :], ms[:, :, :], ACT.Ln))
        act.activation(ms[:, :, :], ms[:, :, :], ACT.Exp, scale=-0.5).then_inc(rstd_ready, 1)

    def vector(dve, _):
        link = Chain(dve, dve_chain)
        for i in range(NS):
            dve.wait_ge(squares, i + 1)
            link(dve.tensor_reduce(ms[:, i, :], sq_v, AX_X, ALU.add))
            dve.tensor_scalar(ms[:, i, :], ms[:, i, :], 1.0 / MLA_D, EPS, ALU.mult, ALU.add).then_inc(mean, 1)
        dve.wait_ge(rstd_ready, 1)
        q_ms = ms[:, 0:2, :].rearrange("p a n -> p (a n)")
        k_ms = ms[:, 2:4, :].rearrange("p a n -> p (a n)")
        link(dve.tensor_tensor(q_all, q_all, head_bcast(q_ms, MLA_D), ALU.mult))
        link(dve.tensor_tensor(k_all[:, :, :HEAD], k_all[:, :, :HEAD], head_bcast(k_ms, HEAD), ALU.mult))
        dve.tensor_tensor(k_raw[:, :, :, HEAD:], kr_rot[:, :, :].unsqueeze(2).to_broadcast([P, TT, HH, ROPE]),
                          k_ms.rearrange("p (t h) -> p t h", h=HH).unsqueeze(3).to_broadcast([P, TT, HH, ROPE]), ALU.mult)
        link(dve.tensor_tensor(q_all[:, :, HEAD:], q_all[:, :, HEAD:],
                               rope_gain[:, 0, :].unsqueeze(1).to_broadcast([P, N, ROPE]), ALU.mult))

        def over_heads(x):
            return x[:, :, :].unsqueeze(2).to_broadcast([P, TT, HH, HR])

        rope(dve, link, over_heads(k.cos), over_heads(k.sin), q_raw[:, :, :, HEAD:], q_raw[:, :, :, HEAD:], tmp)

    return Side(names, scalar, vector)


def lru(k, layer):
    with ExitStack() as s:
        sg = k.sb(s, "lru_gate", [P, CT, SEQ])
        with ExitStack() as s2:
            PAD = CONV_W - 1
            dx = k.sb(s2, "lru_dx", [P, CT, PAD + SEQ])

            def to_dx(i):
                def evac(eng, ps, mn):
                    m, n = mn
                    return eng.tensor_copy(dx[:, 2 * i + m, PAD + n * BANK:PAD + (n + 1) * BANK], ps)
                return ("dve", evac)

            project_block(k, layer, [(C_DX + i * CHUNK, CHUNK, "C", to_dx(i)) for i in range(GROUP_W // CHUNK)],
                          "lru")
            lru_mix(k, layer, s2, dx, sg)
        out_block(k, layer, 3, sg, "lru")


def lru_mix(k, layer, s, dx, sg):
    nc, d = k.nc, k.dram
    names = ["loaded", "zeroed", "blocks_landed", "conv_done", "r_product", "i_product", "r_ready", "i_ready",
             "dve_chain", "act_chain", "handover"]
    (loaded, zeroed, blocks_landed, conv_done, r_product, i_product, r_ready, i_ready, dve_chain, act_chain,
     handover) = map(k.sem, names)
    side_names = ["tau_ready", "square", "u_ready", "root", "dve_chain", "act_chain"]
    tau_ready, square, u_ready, root = map(k.sem, side_names[:4])
    PAD, NH = CONV_W - 1, SEQ // BANK
    xc = k.sb(s, "lru_xc", [P, CT, SEQ])
    r = k.sb(s, "lru_r", [P, CT, SEQ])
    i_g = k.sb(s, "lru_i", [P, CT, SEQ])
    a2 = sg[:, 2:4, :]
    w_bd = [k.sb(s, f"lru_w_{n}", [P, CT, P]) for n in "ri"]
    conv_w = k.sb(s, "lru_conv_w", [P, CONV_W, CT])
    vec = k.sb(s, "lru_vec", [P, 4, CT])
    small = k.sb(s, "lru_small", [P, 4, CT])
    tau = dx
    with nc.Block() as block:
        @block.sync
        def _(sp):
            with nc.allow_non_contiguous_dma(reason="per-channel vectors"):
                for j in range(CONV_W):
                    sp.dma_start(conv_w[:, j, :], d["lru_conv_w"][layer, j, :].rearrange("(m p) -> p m", p=P))\
                      .then_inc(loaded, 16)
                for j, name in enumerate(("lru_conv_b", "lru_b_r", "lru_b_i", "lru_lam")):
                    sp.dma_start(vec[:, j, :], d[name][layer].rearrange("(m p) -> p m", p=P)).then_inc(loaded, 16)
            sp.wait_ge(zeroed, 1)
            for w, name in zip(w_bd, ("lru_w_r", "lru_w_i")):
                src = d[name][layer].rearrange("(m b) c e -> b c m e", b=2)
                for b in range(2):
                    sp.dma_start(w[b * HEAD:(b + 1) * HEAD, :, b * HEAD:(b + 1) * HEAD], src[b]).then_inc(blocks_landed, 16)

        @block.gpsimd
        def _(pool):
            pool.memset(w_bd[0][:, :, :], 0.0)
            pool.memset(w_bd[1][:, :, :], 0.0).then_inc(zeroed, 1)

        @block.tensor
        def _(pe):
            pe.wait_ge(blocks_landed, 64)
            for m in range(CT):
                pe.wait_ge(conv_done, m + 1)
                for n in range(NH):
                    u = m * NH + n
                    for g, (w, done, taken) in enumerate(((w_bd[0], r_product, r_ready), (w_bd[1], i_product, i_ready))):
                        if u >= 4:
                            pe.wait_ge(taken, u - 3)
                        pe.matmul(k.psum[:, 4 * g + u % 4, :], w[:, m, :], xc[:, m, n * BANK:(n + 1) * BANK],
                                  start=True, stop=True).then_inc(done, 1)

        @block.vector
        def _(dve):
            link = Chain(dve, dve_chain)
            link(dve.memset(dx[:, :, :PAD], 0.0))
            dve.wait_ge(loaded, 128)
            link(dve.tensor_scalar(small[:, 0, :], vec[:, 3, :], -1.0, None, ALU.mult))
            dve.tensor_tensor(small[:, 1, :], small[:, 0, :], vec[:, 3, :], ALU.max).then_inc(handover, 1)
            for m in range(CT):
                link(dve.tensor_scalar(xc[:, m, :], dx[:, m, 0:SEQ], conv_w[:, 0, m:m + 1], vec[:, 0, m:m + 1],
                                       ALU.mult, ALU.add))
                for j in range(1, CONV_W):
                    link(dve.scalar_tensor_tensor(out=xc[:, m, :], in0=dx[:, m, j:j + SEQ], scalar=conv_w[:, j, m:m + 1],
                                                  in1=xc[:, m, :], op0=ALU.mult, op1=ALU.add))
                dve.sem_inc(conv_done, 1)
                if m == 0:
                    dve.wait_ge(handover, 2)
                    link(dve.scalar_tensor_tensor(out=small[:, 2, :], in0=small[:, 0, :], scalar=0.0,
                                                  in1=small[:, 1, :], op0=ALU.max, op1=ALU.add))
                    link(dve.tensor_scalar(small[:, 2, :], small[:, 2, :], LRU_C, None, ALU.mult))
                    link(dve.tensor_scalar(small[:, 3, :], small[:, 2, :], -1.0, None, ALU.mult))
            for m in range(CT):
                dve.wait_ge(i_ready, NH * (m + 1))
                dve.wait_ge(r_product, NH * (m + 1))
                dve.wait_ge(i_product, NH * (m + 1))
                link(dve.tensor_tensor(xc[:, m, :], xc[:, m, :], i_g[:, m, :], ALU.mult))

        @block.scalar
        def _(act):
            link = Chain(act, act_chain)
            act.wait_ge(handover, 1)
            link(act.activation(small[:, 1, :], small[:, 1, :], ACT.Exp, scale=-1.0))
            act.activation(small[:, 1, :], small[:, 1, :], ACT.Ln, bias=1.0).then_inc(handover, 1)
            for m in range(CT):
                for n in range(NH):
                    u = m * NH + n
                    at = slice(n * BANK, (n + 1) * BANK)
                    act.wait_ge(r_product, u + 1)
                    act.activation(r[:, m, at], k.psum[:, u % 4, :], ACT.Sigmoid, bias=vec[:, 1, m:m + 1]).then_inc(r_ready, 1)
                    act.wait_ge(i_product, u + 1)
                    act.activation(i_g[:, m, at], k.psum[:, 4 + u % 4, :], ACT.Sigmoid, bias=vec[:, 2, m:m + 1])\
                       .then_inc(i_ready, 1)
            act.wait_ge(i_ready, NH * CT)
    k.clear(names)

    def scalar(act):
        link = Chain(act, act_chain)
        for m in range(CT):
            act.activation(tau[:, m, :SEQ], r[:, m, :], ACT.Tanh, scale=small[:, 2, m:m + 1]).then_inc(tau_ready, 1)
            act.wait_ge(tau_ready, m + 1)
            link(act.activation(r[:, m, :], r[:, m, :], ACT.Exp, scale=small[:, 3, m:m + 1]))
            if m >= 2:
                act.wait_ge(u_ready, m - 1)
            act.activation(a2[:, m % 2, :], r[:, m, :], ACT.Square).then_inc(square, 1)
        for m in range(CT):
            act.wait_ge(u_ready, m + 1)
            act.activation(tau[:, m, :SEQ], tau[:, m, :SEQ], ACT.Sqrt).then_inc(root, 1)

    def vector(dve, _):
        link = Chain(dve, dve_chain)
        for m in range(CT):
            dve.wait_ge(square, m + 1)
            dve.wait_ge(tau_ready, m + 1)
            dve.scalar_tensor_tensor(out=tau[:, m, :SEQ], in0=a2[:, m % 2, :], scalar=1.0, in1=tau[:, m, :SEQ],
                                     op0=ALU.add, op1=ALU.mult).then_inc(u_ready, 1)
        for m in range(CT):
            dve.wait_ge(root, m + 1)
            link(dve.tensor_tensor(xc[:, m, :], xc[:, m, :], tau[:, m, :SEQ], ALU.mult))
            link(dve.tensor_tensor_scan(i_g[:, m, :], r[:, m, :], xc[:, m, :], 0.0, ALU.mult, ALU.add))

    project_block(k, layer, gate_jobs(sg, 3, (0,)), "lru_gate0", side=Side(side_names, scalar, vector))

    def gated(dve, gate_evac):
        dve.tensor_tensor(sg[:, 0:2, :], sg[:, 0:2, :], i_g[:, 0:2, :], ALU.mult)
        for m in (2, 3):
            dve.wait_ge(gate_evac, NH * (m - 1))
            dve.tensor_tensor(sg[:, m, :], sg[:, m, :], i_g[:, m, :], ALU.mult)

    project_block(k, layer, gate_jobs(sg, 3, (1,)), "lru_gate1", side=Side([], lambda act: None, gated))


def store_block(k):
    with k.nc.Block() as block:
        @block.sync
        def _(sp):
            stored = k.sem("stored")
            sp.dma_start(k.out[0].rearrange("(t p) n -> p t n", p=P), k.x[:, :, :]).then_inc(stored, 16)
            sp.wait_ge(stored, 16)


def trunk_kernel(nc, dram, out, parts="ABCD"):
    with ExitStack() as ctx:
        k = Trunk(nc, dram, out, ctx)
        setup_block(k)
        with nc.Fori(0, DEPTH) as layer:
            k.at = 0
            norm_block(k, layer)
            if "A" in parts:
                gla(k, layer)
            if "B" in parts:
                fox(k, layer)
            if "C" in parts:
                mla(k, layer)
            if "D" in parts:
                lru(k, layer)
        store_block(k)


def constants():
    i = np.arange(P)
    masks = np.zeros((P, LEVELS, P // 2), np.int32)
    t = np.arange(P // 2)
    for j in range(LEVELS):
        B = 64 >> j
        masks[:, j, :] = (i[:, None] // (2 * B) == t[None, :] // B) & ((i[:, None] // B) % 2 == 0)
    bf16 = mybir.dt.np(BF16)
    freq = (10000.0 ** (-np.arange(ROPE // 2, dtype=np.float32) / np.float32(ROPE // 2))).astype(np.float32)
    return {
        "c_ident": np.eye(P, dtype=np.float32),
        "c_ident_bf": np.eye(P, dtype=np.float32).astype(bf16),
        "c_mask_bf": np.where(i[:, None] >= i[None, :], 0.0, NEG).astype(np.float32).astype(bf16),
        "c_upper": (i[:, None] <= i[None, :]).astype(np.float32),
        "c_masks": masks,
        "c_head_mask": (i[:, None] // DK == np.arange(HH)[None, :]).astype(np.float32),
        "c_freq": np.tile(freq[None, :], (P, 1)),
    }


_INS = ["x", "positions", "norm_g", "w_in", "w_out", "gla_w_up", "gla_b_up", "gla_g_out", "fox_b_f", "fox_g_q",
        "fox_g_k", "mla_g_cq", "mla_w_uq", "mla_g_ckv", "mla_w_ukv", "mla_g_q", "mla_g_k", "lru_conv_w",
        "lru_conv_b", "lru_w_r", "lru_b_r", "lru_w_i", "lru_b_i", "lru_lam"]


def kernel(**inputs):
    import concourse.bacc as bacc
    from concourse.bass_utils import run_bass_kernel_spmd

    nc = bacc.Bacc("TRN2", target_bir_lowering=False, num_devices=1)
    arrays, dram = {}, {}
    for name, a in list((n, inputs[n]) for n in _INS) + list(constants().items()):
        a = np.ascontiguousarray(a)
        arrays[f"in_{name}_dram"] = a
        dram[name] = nc.dram_tensor(f"in_{name}_dram", a.shape, mybir.dt.from_np(a.dtype), kind="ExternalInput").ap()
    out = nc.dram_tensor("out_0_dram", (1, SEQ, D_MODEL), F32, kind="ExternalOutput").ap()
    trunk_kernel(nc, dram, out)
    r = run_bass_kernel_spmd(nc, [arrays], core_ids=[0])
    return r.results[0]["out_0_dram"]
```
